# Optimizing a Trainium2 kernel written in Bass

```python
import jax, jax.numpy as jnp
from jax import lax
import numpy as np

D_MODEL = 2048
BATCH = 1
SEQ = 256
DEPTH = 1

MEM_LEN = 256
HEAD_DIM = 128
MOBA_HEADS = 8
MOBA_BLOCK = 256
MOBA_TOPK = 3
MOBA_Q_CHUNK = 16
DIL_CONFIGS = ((128, 1), (512, 4), (2048, 16))
DIL_HEADS_PER_GROUP = 4
MEM_HEADS = 4
MEM_HEAD_DIM = 256
ROPE_THETA = 10000.0
RMS_EPS = 1e-6
NEG = -1e30
N_BRANCH = 3

W_A = MOBA_HEADS * HEAD_DIM
W_B_QKV = len(DIL_CONFIGS) * DIL_HEADS_PER_GROUP * HEAD_DIM
W_B_OUT = DIL_HEADS_PER_GROUP * HEAD_DIM
W_M = MEM_HEADS * MEM_HEAD_DIM
IN_SPLITS = (W_A, W_A, W_A, W_A, W_B_QKV, W_B_QKV, W_B_QKV, W_B_OUT, W_M, W_M, N_BRANCH * D_MODEL)
IN_WIDTH = sum(IN_SPLITS)


def rms_norm(x, g):
    xf = x.astype(jnp.float32)
    y = xf * lax.rsqrt(jnp.mean(xf * xf, axis=-1, keepdims=True) + RMS_EPS)
    return (y * g.astype(jnp.float32)).astype(x.dtype)

def rope(x):
    S, D = x.shape[1], x.shape[-1]
    half = D // 2
    inv = ROPE_THETA ** (-jnp.arange(half, dtype=jnp.float32) / half)
    ang = jnp.arange(S, dtype=jnp.float32)[:, None] * inv[None, :]
    cos = jnp.cos(ang)[None, :, None, :]
    sin = jnp.sin(ang)[None, :, None, :]
    xf = x.astype(jnp.float32)
    x1, x2 = xf[..., :half], xf[..., half:]
    return jnp.concatenate([x1 * cos - x2 * sin, x2 * cos + x1 * sin], axis=-1).astype(x.dtype)

def moba_attention(q, k, v):
    B, S, H, D = q.shape
    C = MOBA_Q_CHUNK
    nb = -(-S // MOBA_BLOCK)
    s_pad = nb * MOBA_BLOCK
    scale = D ** -0.5
    qh = q.transpose(0, 2, 1, 3)
    pad = ((0, 0), (0, 0), (0, s_pad - S), (0, 0))
    kb = jnp.pad(k.transpose(0, 2, 1, 3), pad).reshape(B, H, nb, MOBA_BLOCK, D)
    vb = jnp.pad(v.transpose(0, 2, 1, 3), pad).reshape(B, H, nb, MOBA_BLOCK, D)
    k_mean = jnp.mean(kb.astype(jnp.float32), axis=3)
    gate = jnp.einsum('bhsd,bhnd->bhsn', qh.astype(jnp.float32), k_mean)
    q_blk = jnp.arange(S) // MOBA_BLOCK
    past = jnp.arange(nb)[None, :] < q_blk[:, None]
    gate = jnp.where(past[None, None], gate, -jnp.inf)
    n_sel = max(1, min(MOBA_TOPK, nb - 1))
    _, sel = lax.top_k(gate, n_sel)
    sel_valid = jnp.arange(n_sel)[None, :] < q_blk[:, None]

    nq = S // C
    qc = qh.reshape(B, H, nq, C, D).transpose(2, 0, 1, 3, 4)
    selc = sel.reshape(B, H, nq, C, n_sel).transpose(2, 0, 1, 3, 4)
    validc = sel_valid.reshape(nq, C, n_sel)
    bi = jnp.arange(B)[:, None, None, None]
    hi = jnp.arange(H)[None, :, None, None]

    def chunk(args):
        c, q_c, sel_c, valid_c = args
        start = c * C
        own = start // MOBA_BLOCK
        k_own = lax.dynamic_index_in_dim(kb, own, axis=2, keepdims=False)
        v_own = lax.dynamic_index_in_dim(vb, own, axis=2, keepdims=False)
        k_sel = kb[bi, hi, sel_c]
        v_sel = vb[bi, hi, sel_c]
        s_sel = jnp.einsum('bhqd,bhqnkd->bhqnk', q_c, k_sel,
                           preferred_element_type=jnp.float32) * scale
        s_sel = jnp.where(valid_c[None, None, :, :, None], s_sel, NEG)
        s_own = jnp.einsum('bhqd,bhkd->bhqk', q_c, k_own,
                           preferred_element_type=jnp.float32) * scale
        q_pos = start + jnp.arange(C)
        k_pos = own * MOBA_BLOCK + jnp.arange(MOBA_BLOCK)
        s_own = jnp.where(k_pos[None, :] <= q_pos[:, None], s_own, NEG)
        s_all = jnp.concatenate([s_sel.reshape(B, H, C, n_sel * MOBA_BLOCK), s_own], axis=-1)
        p = jax.nn.softmax(s_all, axis=-1)
        p_sel = p[..., :n_sel * MOBA_BLOCK].reshape(B, H, C, n_sel, MOBA_BLOCK).astype(v.dtype)
        p_own = p[..., n_sel * MOBA_BLOCK:].astype(v.dtype)
        return (jnp.einsum('bhqnk,bhqnkd->bhqd', p_sel, v_sel)
                + jnp.einsum('bhqk,bhkd->bhqd', p_own, v_own))

    out = lax.map(chunk, (jnp.arange(nq), qc, selc, validc))
    return out.transpose(1, 0, 3, 2, 4).reshape(B, S, H, D)

def dilated_group(q, k, v, window, dilation):
    B, S, H, D = q.shape
    band = window // dilation
    L = S // dilation
    nblk = -(-L // band)
    Lp = nblk * band
    scale = D ** -0.5

    def to_sub(t):
        t = t.reshape(B, L, dilation, H, D).transpose(0, 2, 3, 1, 4)
        t = jnp.pad(t, ((0, 0), (0, 0), (0, 0), (0, Lp - L), (0, 0)))
        return t.reshape(B, dilation, H, nblk, band, D)

    def with_prev(t):
        prev = jnp.concatenate([jnp.zeros_like(t[:, :, :, :1]), t[:, :, :, :-1]], axis=3)
        return jnp.concatenate([prev, t], axis=4)

    qs, ks, vs = to_sub(q), with_prev(to_sub(k)), with_prev(to_sub(v))
    s = jnp.einsum('brhnqd,brhnkd->brhnqk', qs, ks, preferred_element_type=jnp.float32) * scale
    n_i = jnp.arange(nblk)[:, None, None]
    q_i = jnp.arange(band)[None, :, None]
    k_i = jnp.arange(2 * band)[None, None, :] - band
    delta = q_i - k_i
    mask = (delta >= 0) & (delta <= band) & ((n_i > 0) | (k_i >= 0))
    s = jnp.where(mask, s, NEG)
    m = jnp.max(s, axis=-1, keepdims=True)
    p = jnp.exp(s - m)
    l = jnp.sum(p, axis=-1, keepdims=True)
    o = jnp.einsum('brhnqk,brhnkd->brhnqd', p, vs.astype(jnp.float32)) / l
    lse = (m + jnp.log(l))[..., 0]
    o = o.reshape(B, dilation, H, Lp, D)[:, :, :, :L].transpose(0, 3, 1, 2, 4).reshape(B, S, H, D)
    lse = lse.reshape(B, dilation, H, Lp)[:, :, :, :L].transpose(0, 3, 1, 2).reshape(B, S, H)
    return o, lse

def dilated_mixture(q, k, v):
    B, S, _, D = q.shape
    G = len(DIL_CONFIGS)
    qg = q.reshape(B, S, G, DIL_HEADS_PER_GROUP, D)
    kg = k.reshape(B, S, G, DIL_HEADS_PER_GROUP, D)
    vg = v.reshape(B, S, G, DIL_HEADS_PER_GROUP, D)
    outs, lses = [], []
    for g, (window, dilation) in enumerate(DIL_CONFIGS):
        o, lse = dilated_group(qg[:, :, g], kg[:, :, g], vg[:, :, g], window, dilation)
        outs.append(o)
        lses.append(lse)
    w = jax.nn.softmax(jnp.stack(lses, axis=0), axis=0)
    out = jnp.sum(w[..., None] * jnp.stack(outs, axis=0), axis=0)
    return out.astype(v.dtype)

def memory_attention(q, mk, mv):
    scale = q.shape[-1] ** -0.5
    s = jnp.einsum('bshd,bmhd->bhsm', q, mk, preferred_element_type=jnp.float32) * scale
    p = jax.nn.softmax(s, axis=-1).astype(mv.dtype)
    return jnp.einsum('bhsm,bmhd->bshd', p, mv)

def first_inputs(seed: int = 0) -> dict:
    key = jax.random.key(seed)
    ks = jax.random.split(key, 11)
    f32 = jnp.float32
    x = jax.random.normal(ks[0], (BATCH, SEQ, D_MODEL), f32)
    mem = jax.random.normal(ks[1], (BATCH, MEM_LEN, D_MODEL), f32)
    norm_in_g = 1.0 + 0.05 * jax.random.normal(ks[2], (DEPTH, D_MODEL), f32)
    norm_mem_g = 1.0 + 0.05 * jax.random.normal(ks[3], (D_MODEL,), f32)
    w_in = jax.random.normal(ks[4], (DEPTH, D_MODEL, IN_WIDTH), f32) * D_MODEL ** -0.5
    w_mem_kv = jax.random.normal(ks[5], (DEPTH, D_MODEL, 2 * W_M), f32) * D_MODEL ** -0.5
    w_proj_a = jax.random.normal(ks[6], (DEPTH, W_A, D_MODEL), f32) * W_A ** -0.5
    w_proj_b = jax.random.normal(ks[7], (DEPTH, W_B_OUT, D_MODEL), f32) * W_B_OUT ** -0.5
    w_proj_m = jax.random.normal(ks[8], (DEPTH, W_M, D_MODEL), f32) * W_M ** -0.5
    w_out = jax.random.normal(ks[9], (DEPTH, D_MODEL, D_MODEL), f32) * D_MODEL ** -0.5
    norm_final_g = 1.0 + 0.05 * jax.random.normal(ks[10], (D_MODEL,), f32)
    return {"x": x, "mem": mem, "norm_in_g": norm_in_g, "norm_mem_g": norm_mem_g,
            "w_in": w_in, "w_mem_kv": w_mem_kv, "w_proj_a": w_proj_a, "w_proj_b": w_proj_b,
            "w_proj_m": w_proj_m, "w_out": w_out, "norm_final_g": norm_final_g}

def first_block(x, mem, norm_in_g, norm_mem_g, w_in, w_mem_kv, w_proj_a, w_proj_b, w_proj_m,
              w_out, norm_final_g):
    B, S, _ = x.shape
    M = mem.shape[1]
    split_points = [int(p) for p in np.cumsum(IN_SPLITS)[:-1]]
    mem_n = rms_norm(mem, norm_mem_g)
    for layer in range(DEPTH):
        h = rms_norm(x, norm_in_g[layer])
        proj = jnp.einsum('bsd,de->bse', h, w_in[layer])
        (qa, ka, va, za, qb, kb, vb, zb, qm, zm, gates) = jnp.split(proj, split_points, axis=-1)

        qa = rope(qa.reshape(B, S, MOBA_HEADS, HEAD_DIM))
        ka = rope(ka.reshape(B, S, MOBA_HEADS, HEAD_DIM))
        va = va.reshape(B, S, MOBA_HEADS, HEAD_DIM)
        ya = moba_attention(qa, ka, va).reshape(B, S, W_A) * jax.nn.silu(za)

        hb = len(DIL_CONFIGS) * DIL_HEADS_PER_GROUP
        qb = rope(qb.reshape(B, S, hb, HEAD_DIM))
        kb = rope(kb.reshape(B, S, hb, HEAD_DIM))
        vb = vb.reshape(B, S, hb, HEAD_DIM)
        yb = dilated_mixture(qb, kb, vb).reshape(B, S, W_B_OUT) * jax.nn.silu(zb)

        mkv = jnp.einsum('bmd,de->bme', mem_n, w_mem_kv[layer])
        mk, mv = jnp.split(mkv, 2, axis=-1)
        ym = memory_attention(qm.reshape(B, S, MEM_HEADS, MEM_HEAD_DIM),
                              mk.reshape(B, M, MEM_HEADS, MEM_HEAD_DIM),
                              mv.reshape(B, M, MEM_HEADS, MEM_HEAD_DIM)).reshape(B, S, W_M)
        ym = ym * jax.nn.silu(zm)

        g_a, g_b, g_m = jnp.split(jax.nn.sigmoid(gates), N_BRANCH, axis=-1)
        merged = (g_a * jnp.einsum('bse,ed->bsd', ya, w_proj_a[layer])
                  + g_b * jnp.einsum('bse,ed->bsd', yb, w_proj_b[layer])
                  + g_m * jnp.einsum('bse,ed->bsd', ym, w_proj_m[layer]))
        x = x + jnp.einsum('bsd,de->bse', merged, w_out[layer])
    return rms_norm(x, norm_final_g)


D_MIX = D_MODEL
D_LRU = D_MIX // 2
D_RET = D_MIX - D_LRU
LRU_BLOCKS = 8
LRU_BLOCK_W = D_LRU // LRU_BLOCKS
CONV_W = 4
LRU_C = 8.0
RET_HEADS = 8
RET_HD = D_RET // RET_HEADS
CHUNK = 128
ROPE_BASE = 10000.0
D_FF = ((8 * D_MODEL + 3 * 256 - 1) // (3 * 256)) * 256
EPS = 1e-6
SPLITS = (D_LRU, 2 * D_LRU, 2 * D_LRU + D_RET, 2 * D_LRU + 2 * D_RET, 2 * D_LRU + 3 * D_RET)
D_IN = 2 * D_LRU + 4 * D_RET


def rmsnorm(x, w):
    xf = x.astype(jnp.float32)
    y = xf * lax.rsqrt(jnp.mean(xf * xf, axis=-1, keepdims=True) + EPS)
    return (y * w.astype(jnp.float32)).astype(x.dtype)

def causal_depthwise_conv(x, w, b):
    S = x.shape[1]
    xp = jnp.pad(x, ((0, 0), (CONV_W - 1, 0), (0, 0)))
    y = b
    for tap in range(CONV_W):
        y = y + xp[:, tap:tap + S, :] * w[tap]
    return y

def rg_lru(u, wa, ba, wx, bx, lam):
    B, S, _ = u.shape
    uf = u.astype(jnp.float32)
    ub = uf.reshape(B, S, LRU_BLOCKS, LRU_BLOCK_W)
    r = jax.nn.sigmoid(jnp.einsum('bsnc,ncd->bsnd', ub, wa.astype(jnp.float32)).reshape(B, S, D_LRU) + ba)
    i = jax.nn.sigmoid(jnp.einsum('bsnc,ncd->bsnd', ub, wx.astype(jnp.float32)).reshape(B, S, D_LRU) + bx)
    log_a = LRU_C * r * jax.nn.log_sigmoid(lam.astype(jnp.float32))
    a = jnp.exp(log_a)
    b = jnp.sqrt(-jnp.expm1(2.0 * log_a)) * (i * uf)

    def combine(left, right):
        a1, b1 = left
        a2, b2 = right
        return a1 * a2, a2 * b1 + b2

    _, h = lax.associative_scan(combine, (a, b), axis=1)
    return h.astype(u.dtype)

def rope_2(t, cos, sin):
    half = t.shape[-1] // 2
    t1, t2 = t[..., :half], t[..., half:]
    c = cos[None, :, None, :]
    s = sin[None, :, None, :]
    return jnp.concatenate([t1 * c - t2 * s, t1 * s + t2 * c], axis=-1)

def retention(q, k, v, g, gn_w):
    B, S, _ = q.shape
    H, Dh, C = RET_HEADS, RET_HD, CHUNK
    N = S // C
    f32 = jnp.float32
    pos = jnp.arange(S, dtype=f32)
    inv_freq = ROPE_BASE ** (-jnp.arange(0, Dh, 2, dtype=f32) / Dh)
    ang = pos[:, None] * inv_freq[None, :]
    cos, sin = jnp.cos(ang), jnp.sin(ang)
    qh = rope_2(q.astype(f32).reshape(B, S, H, Dh), cos, sin)
    kh = rope_2(k.astype(f32).reshape(B, S, H, Dh), cos, sin) * (Dh ** -0.5)
    vh = v.astype(f32).reshape(B, S, H, Dh)
    qc = qh.reshape(B, N, C, H, Dh)
    kc = kh.reshape(B, N, C, H, Dh)
    vc = vh.reshape(B, N, C, H, Dh)

    log_gamma = jnp.log1p(-jnp.exp2(-5.0 - jnp.arange(H, dtype=f32)))
    idx = jnp.arange(C)
    diff = idx[:, None] - idx[None, :]
    causal = diff >= 0
    decay = jnp.where(causal[None], jnp.exp(log_gamma[:, None, None] * jnp.where(causal, diff, 0)[None].astype(f32)), 0.0)

    scores = jnp.einsum('bnqhd,bnkhd->bnhqk', qc, kc) * decay[None, None]
    inner = jnp.einsum('bnhqk,bnkhe->bnqhe', scores, vc)

    zeta = jnp.exp(log_gamma[None, :] * (C - 1 - idx).astype(f32)[:, None])
    kv = jnp.einsum('bnkhd,bnkhe->bnhde', kc * zeta[:, :, None], vc)
    chunk_decay = jnp.exp(log_gamma * C)[:, None, None]

    def step(R, kv_n):
        return R * chunk_decay + kv_n, R

    _, R_prev = lax.scan(step, jnp.zeros((B, H, Dh, Dh), f32), jnp.moveaxis(kv, 1, 0))
    R_prev = jnp.moveaxis(R_prev, 0, 1)

    xi = jnp.exp(log_gamma[None, :] * (idx + 1).astype(f32)[:, None])
    cross = jnp.einsum('bnqhd,bnhde->bnqhe', qc * xi[:, :, None], R_prev)
    o = (inner + cross).reshape(B, S, H, Dh)

    mu = jnp.mean(o, axis=-1, keepdims=True)
    var = jnp.mean(jnp.square(o - mu), axis=-1, keepdims=True)
    on = ((o - mu) * lax.rsqrt(var + EPS)).reshape(B, S, D_RET) * gn_w.astype(f32)
    return (jax.nn.silu(g.astype(f32)) * on).astype(q.dtype)

def second_inputs(seed: int = 0) -> dict:
    key = jax.random.key(seed)
    ks = jax.random.split(key, 20)
    f32 = jnp.float32

    def nrm(k, shape, scale):
        return jax.random.normal(k, shape, f32) * scale

    u = jax.random.uniform(ks[8], (DEPTH, D_LRU), f32, 0.9, 0.999)
    s = u ** (1.0 / LRU_C)
    lru_lambda = jnp.log(s) - jnp.log1p(-s)
    return {
        "x": nrm(ks[0], (BATCH, SEQ, D_MODEL), 1.0),
        "ln1_w": 1.0 + nrm(ks[1], (DEPTH, D_MODEL), 0.02),
        "w_in": nrm(ks[2], (DEPTH, D_MODEL, D_IN), D_MODEL ** -0.5),
        "conv_w": nrm(ks[3], (DEPTH, CONV_W, D_LRU), CONV_W ** -0.5),
        "conv_b": nrm(ks[4], (DEPTH, D_LRU), 0.01),
        "gate_a_w": nrm(ks[5], (DEPTH, LRU_BLOCKS, LRU_BLOCK_W, LRU_BLOCK_W), LRU_BLOCK_W ** -0.5),
        "gate_a_b": nrm(ks[6], (DEPTH, D_LRU), 0.01),
        "gate_x_w": nrm(ks[7], (DEPTH, LRU_BLOCKS, LRU_BLOCK_W, LRU_BLOCK_W), LRU_BLOCK_W ** -0.5),
        "gate_x_b": nrm(ks[9], (DEPTH, D_LRU), 0.01),
        "lru_lambda": lru_lambda,
        "ret_gn_w": 1.0 + nrm(ks[10], (DEPTH, D_RET), 0.02),
        "w_out": nrm(ks[11], (DEPTH, D_MIX, D_MODEL), D_MIX ** -0.5),
        "ln2_w": 1.0 + nrm(ks[12], (DEPTH, D_MODEL), 0.02),
        "w_ffn_gate": nrm(ks[13], (DEPTH, D_MODEL, D_FF), D_MODEL ** -0.5),
        "w_ffn_up": nrm(ks[14], (DEPTH, D_MODEL, D_FF), D_MODEL ** -0.5),
        "w_ffn_down": nrm(ks[15], (DEPTH, D_FF, D_MODEL), D_FF ** -0.5),
        "final_norm_w": 1.0 + nrm(ks[16], (D_MODEL,), 0.02),
    }

def second_block(x, ln1_w, w_in, conv_w, conv_b, gate_a_w, gate_a_b, gate_x_w, gate_x_b,
              lru_lambda, ret_gn_w, w_out, ln2_w, w_ffn_gate, w_ffn_up, w_ffn_down, final_norm_w):
    h = x
    for l in range(DEPTH):
        u = rmsnorm(h, ln1_w[l])
        proj = jnp.einsum('bsd,de->bse', u, w_in[l])
        lru_x, lru_g, q, k, v, ret_g = jnp.split(proj, SPLITS, axis=-1)
        lru_x = causal_depthwise_conv(lru_x, conv_w[l], conv_b[l])
        y_lru = rg_lru(lru_x, gate_a_w[l], gate_a_b[l], gate_x_w[l], gate_x_b[l], lru_lambda[l])
        y_lru = y_lru * jax.nn.gelu(lru_g)
        y_ret = retention(q, k, v, ret_g, ret_gn_w[l])
        y = jnp.concatenate([y_lru, y_ret], axis=-1)
        h = h + jnp.einsum('bse,ed->bsd', y, w_out[l])
        u = rmsnorm(h, ln2_w[l])
        ff = jax.nn.silu(jnp.einsum('bsd,df->bsf', u, w_ffn_gate[l])) * jnp.einsum('bsd,df->bsf', u, w_ffn_up[l])
        h = h + jnp.einsum('bsf,fd->bsd', ff, w_ffn_down[l])
    return rmsnorm(h, final_norm_w)


def setup_inputs(seed=0):
    out = dict(first_inputs(seed))
    for name, value in second_inputs(seed + 1).items():
        if name != "x":
            out[name + "_2"] = value
    return out


def reference(
    x, mem, norm_in_g, norm_mem_g, w_in, w_mem_kv, w_proj_a, w_proj_b, w_proj_m, w_out,
    norm_final_g, ln1_w_2, w_in_2, conv_w_2, conv_b_2, gate_a_w_2, gate_a_b_2, gate_x_w_2,
    gate_x_b_2, lru_lambda_2, ret_gn_w_2, w_out_2, ln2_w_2, w_ffn_gate_2, w_ffn_up_2,
    w_ffn_down_2, final_norm_w_2,
):
    x = first_block(
        x, mem, norm_in_g, norm_mem_g, w_in, w_mem_kv, w_proj_a, w_proj_b, w_proj_m, w_out,
        norm_final_g,
    )
    return second_block(
        x, ln1_w_2, w_in_2, conv_w_2, conv_b_2, gate_a_w_2, gate_a_b_2, gate_x_w_2, gate_x_b_2,
        lru_lambda_2, ret_gn_w_2, w_out_2, ln2_w_2, w_ffn_gate_2, w_ffn_up_2, w_ffn_down_2,
        final_norm_w_2,
    )


_drawn_inputs = setup_inputs


def setup_inputs(seed=0):
    import zlib

    import numpy as np

    out = dict(_drawn_inputs(seed))
    spreads = {}
    factors = {'norm_in_g': 4.155,
     'norm_mem_g': 8.0,
     'ln1_w_2': 2.993,
     'conv_b_2': 9.186,
     'gate_a_b_2': 64.0,
     'gate_x_b_2': 64.0,
     'ret_gn_w_2': 6.805,
     'ln2_w_2': 3.998,
     'final_norm_w_2': 7.622}
    for name, (base, spread) in spreads.items():
        noise = np.random.default_rng([zlib.crc32(name.encode()), seed]).standard_normal(out[name].shape)
        drawn = base * np.exp(spread * noise) if base else spread * noise
        out[name] = __import__('jax').numpy.asarray(drawn.astype(out[name].dtype))
    for name, factor in factors.items():
        out[name] = (out[name] * factor).astype(out[name].dtype)
    return out
```

```python
from contextlib import ExitStack

import numpy as np

import concourse.bass as bass
from concourse import mybir

ALU = mybir.AluOpType
ACT = mybir.ActivationFunctionType
F32 = mybir.dt.float32
F32R = mybir.dt.float32r
BF16 = mybir.dt.bfloat16
AX = mybir.AxisListType.X

P = 128
S = 256
NT = S // P
D = 2048
KC = D // P
NW = 512
HD = 128
EPS = 1e-6
SLOTS = 4
KIB = 1024
SBUF0 = 16640
QUAD = NW // HD

C_ID, C_COS, C_SIN, C_MASK = 0, 128, 256, 512
C_END = C_MASK + 8 * P
M_NONE, M_CAUSAL, M_DIL = 0, 1, 2

V_MEM, V_IN, V_LN1, V_LN2, V_GN, V_CONVW, V_CONVB, V_GAB, V_GXB, V_LAM, V_END = (
    0, 16, 32, 48, 64, 72, 104, 112, 120, 128, 136)


class Walk:

    NAMES = ("g", "a0", "a1", "z", "st", "j0", "j1", "h0", "h1", "norm", "u", "link")

    def __init__(self):
        self.n = dict.fromkeys(self.NAMES, 0)
        self.loop = None

    def __call__(self, name, plus=0):
        if self.loop is None or not self.loop[1][name]:
            return self.n[name] + plus
        i, per = self.loop
        return i * per[name] + (self.n[name] + plus)

    def slot_uses(self):
        uses = 16 * (self.n["g"] // SLOTS + 1)
        return uses if self.loop is None else self.loop[0] * (16 * self.loop[1]["g"] // SLOTS) + uses

    def step(self, *names):
        for name in names:
            self.n[name] += 1

    def rounds(self, eng, count, body):
        before = dict(self.n)
        body(0)
        per = {k: self.n[k] - before[k] for k in self.n}
        assert per["g"] % SLOTS == 0
        if count > 1:
            self.n = dict(before)
            with eng.Fori(1, count) as i:
                self.loop = (i, per)
                body(i)
            self.loop = None
        self.n = {k: before[k] + count * per[k] for k in before}

    def count_post(self, prev):
        kind = prev["post"]
        if not through_stage(kind):
            self.step(f"a{prev['par']}")
        if kind[0] in ("silu", "ffg"):
            self.step("z")

    def count_job(self, prev):
        if through_stage(prev["post"]):
            self.step("st", "j0", *(("h0",) if split_job(prev["post"]) else ()))


def through_stage(kind):
    return kind[0] in ("turn", "rope", "ffu") or kind[0] == "mix" and kind[2] == "last"


def split_job(kind):
    return kind[0] in ("ffu", "mix")


def build(nc, x, mem, w_in, w_mkv, w_pa, w_pb, w_pm, w_out, fin1_g, w_in2, w_out2, w_gate, w_up, w_down,
          fin2_g, gate_a, gate_x, vecs, consts_d, decay_d, spill, out):
    ctx = ExitStack()
    with ctx:
        def at(name, shape, dt, kib):
            return nc.alloc_sbuf_tensor_at(name, shape, dt, offset=SBUF0 + int(kib * KIB))

        def sem(name):
            return ctx.enter_context(nc.semaphore(name))

        raw = at("raw", [P, SLOTS, 2, NW], F32, 0)
        w_hi = at("w_hi", [P, SLOTS, 2, NW], F32R, 16)
        w_lo = at("w_lo", [P, SLOTS, 2, NW], F32R, 32)
        xT_hi = at("xT_hi", [P, KC, S], F32R, 48)
        xT_lo = at("xT_lo", [P, KC, S], F32R, 64)
        memT_hi = at("memT_hi", [P, KC, S], F32R, 80)
        memT_lo = at("memT_lo", [P, KC, S], F32R, 96)
        yT_hi = at("yT_hi", [P, 20, S], F32R, 80)
        yT_lo = at("yT_lo", [P, 20, S], F32R, 100)
        x_tok = at("x_tok", [P, NT, D], F32, 120)
        mem_tok = at("mem_tok", [P, NT, D], F32, 136)
        qmT = at("qmT", [P, 8, S], F32, 136)
        zm = at("zm", [P, NT, 1024], F32, 144)
        mv = at("mv", [P, NT, 1024], F32, 152)
        mkT = at("mkT", [P, 8, S], F32, 160)
        half_at = (120, 160)
        qaT, kaT, va, za = (
            [at(f"{n}{h}", s, F32, half_at[h] + 4 * m) for h in range(2)]
            for m, (n, s) in enumerate((("qaT", [P, QUAD, S]), ("kaT", [P, QUAD, S]), ("va", [P, NT, NW]), ("za", [P, NT, NW]))))
        qbT = at("qbT", [P, 12, S], F32, 120)
        kbT = at("kbT", [P, 12, S], F32, 132)
        vb = at("vb", [P, 3, NT, NW], F32, 144)
        zb = at("zb", [P, NT, NW], F32, 156)
        gates = at("gates", [P, 3, NT, NW], F32, 160)
        mrgT_hi = at("mrgT_hi", [P, KC, S], F32R, 120)
        mrgT_lo = at("mrgT_lo", [P, KC, S], F32R, 136)
        x1 = at("x1", [P, NT, D], F32, 48)
        u_tok = at("u_tok", [P, NT, D], F32, 64)
        uT_hi = at("uT_hi", [P, KC, S], F32R, 80)
        uT_lo = at("uT_lo", [P, KC, S], F32R, 96)
        lxT = at("lxT", [P, 8, S], F32, 64)
        lgT = at("lgT", [P, 8, S], F32, 72)
        decay = at("decay", [P, 8, S], F32, 112)
        ret_at = (120, 136)
        qrT, krT, vr, gr = (
            [at(f"{n}{h}", s, F32, ret_at[h] + 4 * m) for h in range(2)]
            for m, (n, s) in enumerate((("qrT", [P, QUAD, S]), ("krT", [P, QUAD, S]), ("vr", [P, NT, NW]), ("gr", [P, NT, NW]))))
        ga_w = at("ga_w", [P, 8, P], F32, 152)
        gx_w = at("gx_w", [P, 8, P], F32, 156)
        y2T_hi = at("y2T_hi", [P, KC, S], F32R, 48)
        y2T_lo = at("y2T_lo", [P, KC, S], F32R, 160)
        h2 = at("h2", [P, NT, D], F32, 92)
        u2T_hi = at("u2T_hi", [P, KC, S], F32R, 108)
        u2T_lo = at("u2T_lo", [P, KC, S], F32R, 124)
        u2_tok = at("u2_tok", [P, NT, D], F32, 140)
        FC = w_down.shape[0] // P
        ffT_lo = at("ffT_lo", [P, FC, S], F32R, 48)
        ffT_hi = at("ffT_hi", [P, FC, S], F32R, 140)
        g_row1 = at("g_row1", [P, D], F32, 176)
        g_row2 = at("g_row2", [P, D], F32, 108)
        scores = at("scores", [P, 1152], F32, 176)
        probsT = at("probsT", [P, 1152], F32, 180.5)
        consts = at("consts", [P, C_END], F32, 185)
        ident = consts[:, C_ID:C_ID + P]
        lt_a = at("lt_a", [P, 4, S], F32, 176)
        lt_b = at("lt_b", [P, 4, S], F32, 187)
        lru_u, lru_t, lru_i, lru_r = (lt_a[:, k] for k in range(4))
        lru_a, lru_root_, lru_y, gelu = (lt_b[:, k] for k in range(4))
        stage = at("stage", [P, NT, NW], F32, 191)
        tmp = at("tmp", [P, NT, NW], F32, 195)
        sq_out = at("sq_out", [P, D], BF16, 195)
        y_tok = at("y_tok", [P, NT, S], F32, 199)
        ff_g = at("ff_g", [P, NT, NW], F32, 186)
        cols = at("cols", [P, V_END], F32, 201)
        vec_a = at("vec_a", [P, P], F32, 202)
        vec_b = at("vec_b", [P, P], F32, 202.5)
        small = at("small", [P, 128], F32, 203)
        lamb = at("lamb", [P, 8, 8], F32, 203.5)
        half_c = at("half_c", [P, S], F32, 203.75)
        mneg_c = at("mneg_c", [P, 2], F32, 204.75)

        rowmax, negmax, rowsum, rinv = (small[:, k:k + 2] for k in (0, 2, 4, 6))
        sumsq, meansq, rstd = (small[:, k:k + 2] for k in (8, 10, 12))
        stats = small[:, 16:28].rearrange("p (t s) -> p t s", t=2)
        moments = small[:, 28:32].rearrange("p (t s) -> p t s", t=2)
        ret_rstd = small[:, 32:34]
        ret_var = small[:, 34:36]
        gn_half = small[:, 40:48]
        gab_half = small[:, 48:64]
        gxb_half = small[:, 56:64]
        ls4 = small[:, 64:72]
        lam = cols[:, V_LAM:V_LAM + 8]

        ps = ctx.enter_context(nc.psum_tensor("ps", [P, 8 * NW], F32))

        def bank(b, lo=0, hi=NW):
            return ps[:, b * NW + lo:b * NW + hi]

        raw_in = [sem(f"raw_in{k}") for k in range(SLOTS)]
        hi_ready = sem("hi_ready")
        lo_ready = sem("lo_ready")
        w_used = sem("w_used")
        acc_free = [sem("acc_free0"), sem("acc_free1")]
        z_tanh = sem("z_tanh")
        st_ready = sem("st_ready")
        tx_done = [sem("tx_done0"), sem("tx_done1")]
        tx_hi = [sem("tx_hi0"), sem("tx_hi1")]
        tx_free = [sem("tx_free0"), sem("tx_free1")]
        u_score, u_max, u_exp, u_pT, u_pTc, u_out, u_y, u_yT, u_hi, u_lo = (
            sem(n) for n in ("u_score", "u_max", "u_exp", "u_pT", "u_pTc", "u_out", "u_y", "u_yT", "u_hi", "u_lo"))
        r_score, r_dec, r_out, r_var, r_rstd, r_y, r_yT, r_hi, r_lo = (
            sem(n) for n in ("r_score", "r_dec", "r_out", "r_var", "r_rstd", "r_y", "r_yT", "r_hi", "r_lo"))
        l_sq, l_arg, l_conv, l_gate, l_own, l_tanh, l_nt, l_sqrt, l_y, l_hi, l_lo = (
            sem(n) for n in ("l_sq", "l_arg", "l_conv", "l_gate", "l_own", "l_tanh", "l_nt", "l_sqrt", "l_y", "l_hi", "l_lo"))
        n_sum, n_mean, n_rstd, n_ready = sem("n_sum"), sem("n_mean"), sem("n_rstd"), sem("n_ready")
        dve_link = sem("dve_link")
        in_mem = [sem("in_mem0"), sem("in_mem1")]
        in_x = [sem("in_x0"), sem("in_x1")]
        in_const, in_vec, in_res, in_g1, in_dec, in_gw, in_g2 = (
            sem(n) for n in ("in_const", "in_vec", "in_res", "in_g1", "in_dec", "in_gw", "in_g2"))
        spilled, in_h2, stored = sem("spilled"), sem("in_h2"), sem("stored")
        x_added = sem("x_added")
        pool_c, vec_ps, cols_ready, lam_abs, lam_e, lam_ready = (
            sem(n) for n in ("pool_c", "vec_ps", "cols_ready", "lam_abs", "lam_e", "lam_ready"))

        A0, B0 = 0, 4 * 1024
        QB, KB, VB, ZB = B0, B0 + 1536, B0 + 3072, B0 + 4608
        QM, ZM, GT = ZB + 512, ZB + 512 + 1024, ZB + 512 + 2048
        NG = D // NW
        NF = w_gate.shape[1] // NW

        def mem_unit(h):
            src = ([(qmT, 2 * h + c) for c in range(2)], [(mkT, 2 * h + c) for c in range(2)],
                   lambda kt: mv[:, kt, h * 256:(h + 1) * 256])
            return dict(scale=256 ** -0.5, blocks=[[(src, 0), (src, 1)]] * 2, mask=None, width=256,
                        s_at=(6 * NW, 6 * NW + 256), p_at=(7 * NW, 7 * NW + 256), o_at=6 * NW, y_at=7 * NW,
                        z=lambda t: zm[:, t, h * 256:(h + 1) * 256], kc=12 + 2 * h)

        def moba_unit(n):
            half, h = n // QUAD, n % QUAD
            src = ([(qaT[half], h)], [(kaT[half], h)], lambda kt: va[half][:, kt, h * HD:(h + 1) * HD])
            return dict(scale=HD ** -0.5, blocks=[[(src, 0)], [(src, 0), (src, 1)]], width=HD,
                        mask=(M_CAUSAL, M_NONE), s_at=(6 * NW, 6 * NW + P), p_at=(7 * NW, 7 * NW + P),
                        o_at=6 * NW, y_at=7 * NW, z=lambda t: za[half][:, t, h * HD:(h + 1) * HD], kc=n)

        def dil_unit(j):
            srcs = [([(qbT, g * QUAD + j)], [(kbT, g * QUAD + j)],
                     lambda kt, g=g: vb[:, g, kt, j * HD:(j + 1) * HD]) for g in range(3)]
            return dict(scale=HD ** -0.5, blocks=[[(s, 0) for s in srcs], [(s, kt) for s in srcs for kt in range(2)]],
                        width=HD, mask=("dil0", "dil1"), s_at=(4 * NW, 5 * NW), p_at=(4 * NW, 5 * NW),
                        o_at=7 * NW, y_at=4 * NW, z=lambda t: zb[:, t, j * HD:(j + 1) * HD], kc=8 + j, dil=True)

        def sb_at(unit, t):
            w0 = P * len(unit["blocks"][0])
            return (0, w0)[t], P * len(unit["blocks"][t])

        def masks(unit, t):
            m = unit["mask"][t]
            tiles = consts[:, C_MASK:C_END].rearrange("p (m c) -> p m c", c=P)
            if m == "dil0":
                return tiles[:, M_DIL + 1:M_DIL + 6:2, :]
            if m == "dil1":
                return tiles[:, M_DIL:M_DIL + 6, :]
            n = len(unit["blocks"][t])
            return tiles[:, m:m + n, :]

        def tiles_memkv():
            return [dict(w=w_mkv, col=NW * n, x="mem", post=("turn", mkT, n * QUAD) if n < 2 else ("take", mv[:, :, (n - 2) * NW:(n - 1) * NW]))
                    for n in range(4)]

        def tiles_attention():
            out_ = [dict(w=w_in, col=QM + NW * n, x="x", post=("turn", qmT, n * QUAD)) for n in range(2)]
            out_ += [dict(w=w_in, col=ZM + NW * n, x="x", post=("silu", zm[:, :, n * NW:(n + 1) * NW])) for n in range(2)]
            for half in range(2):
                c = A0 + half * NW
                four = [dict(w=w_in, col=c, x="x", post=("rope", qaT[half], 0)),
                        dict(w=w_in, col=c + 1024, x="x", post=("rope", kaT[half], 0)),
                        dict(w=w_in, col=c + 2048, x="x", post=("take", va[half][:, :, :])),
                        dict(w=w_in, col=c + 3072, x="x", post=("silu", za[half][:, :, :]))]
                for n in range(4):
                    four[n]["unit"] = mem_unit(n) if half == 0 else moba_unit(n)
                out_ += four
            ten = [dict(w=w_in, col=QB + NW * g, x="x", post=("rope", qbT, g * QUAD)) for g in range(3)]
            ten += [dict(w=w_in, col=KB + NW * g, x="x", post=("rope", kbT, g * QUAD)) for g in range(3)]
            ten += [dict(w=w_in, col=VB + NW * g, x="x", post=("take", vb[:, g])) for g in range(3)]
            ten += [dict(w=w_in, col=ZB, x="x", post=("silu", zb[:, :, :]))]
            for n in range(4):
                ten[n]["unit"] = moba_unit(QUAD + n)
            return out_ + ten

        def tiles_merge(n, first=False):
            out_ = [dict(w=w_in, col=n * NW + (GT + b * D), x="x", post=("gate", b)) for b in (2, 0, 1)]
            out_ += [dict(w=w_pm, col=n * NW, x="y", k0=12, hcs=4, post=("mix", 2, "first")),
                     dict(w=w_pa, col=n * NW, x="y", k0=0, hcs=4, post=("mix", 0, "more")),
                     dict(w=w_pb, col=n * NW, x="y", k0=8, hcs=4, per=1, post=("mix", 1, "last", n))]
            if first:
                for k in range(4):
                    out_[k]["unit"] = dil_unit(k)
            return out_

        def tiles_two():
            out_ = []
            for half in range(2):
                out_ += [dict(w=w_in2, col=half * NW, x="u", post=("turn", lxT, half * QUAD)),
                         dict(w=w_in2, col=1024 + half * NW, x="u", post=("turn", lgT, half * QUAD))]
            for half in range(2):
                c = 2048 + half * NW
                out_ += [dict(w=w_in2, col=c, x="u", post=("rope", qrT[half], 0)),
                         dict(w=w_in2, col=c + 1024, x="u", post=("rope", krT[half], 0)),
                         dict(w=w_in2, col=c + 2048, x="u", post=("take", vr[half][:, :, :])),
                         dict(w=w_in2, col=c + 3072, x="u", post=("silu", gr[half][:, :, :]))]
            for n in range(8):
                out_[4 + n]["lru"] = n
            for n in range(4):
                out_[8 + n]["ret"] = n
            return out_

        def tiles_ffn(n):
            return [dict(w=w_gate, col=n * NW, x="u2", post=("ffg",)),
                    dict(w=w_up, col=n * NW, x="u2", post=("ffu", n))]

        def merge_last(n):
            return dict(post=("mix", 1, "last", n), par=1)

        def ffn_last(n):
            return dict(post=("ffu", n), par=1)

        HCS = 8
        PARTS = {"mem": (memT_hi, memT_lo), "x": (xT_hi, xT_lo), "y": (yT_hi, yT_lo), "m": (mrgT_hi, mrgT_lo),
                 "u": (uT_hi, uT_lo), "y2": (y2T_hi, y2T_lo), "u2": (u2T_hi, u2T_lo), "ff": (ffT_hi, ffT_lo)}

        def pos(tile, p):
            return min(p, tile.get("hcs", HCS) - 1)

        def res_tiles(weight, x, dst, k=0, hcs=HCS):
            return [dict(w=weight, col=(k * 2 + m) * NW, x=x, hcs=hcs, post=("res", dst, k * 2 + m)) for m in range(2)]

        G_X = 8 * 26 + 36 * (NG - 1) + 24
        G_U = 8 * 26 + 36 * NG + 8 * NG + 8 * 12
        G_U2 = G_U + 8 * NG + 16 * NF

        block = ctx.enter_context(nc.Block())

        @block.sync
        def _(sp):
            w = Walk()

            def load(tile):
                per, hcs = tile.get("per", 2), tile.get("hcs", HCS)
                src = tile["w"].rearrange("(c p) n -> p c n", p=P)
                if w.loop:
                    sp.to_reg(tile["col"] * 4)
                for h in range(hcs):
                    s = w.n["g"] % SLOTS
                    sp.wait_ge(lo_ready, w("g", 1))
                    sp.dma_start(raw[:, s, 0:per], src[:, h * per:(h + 1) * per, bass.ds(tile["col"], NW)])\
                      .then_inc(raw_in[s], 16)
                    w.step("g")

            def load_all(tiles):
                for tile in tiles:
                    load(tile)

            for t in range(NT):
                sp.dma_start(mem_tok[:, t], mem[t * P:(t + 1) * P, :]).then_inc(in_mem[t], 16)
            sp.dma_start(vec_a[:, :], vecs[0:P]).then_inc(in_vec, 16)
            sp.dma_start(vec_b[0:V_END - P, :], vecs[P:V_END]).then_inc(in_vec, 16)
            sp.dma_start(consts[:, :], consts_d).then_inc(in_const, 16)
            first, *rest = tiles_memkv()
            load(first)
            for t in range(NT):
                sp.dma_start(x_tok[:, t], x[t * P:(t + 1) * P, :]).then_inc(in_x[t], 16)
            load_all(rest + tiles_attention() + tiles_merge(0))
            w.rounds(sp, NG - 1, lambda i: load_all(tiles_merge(i + 1)))
            w.rounds(sp, NG // 2, lambda i: load_all(res_tiles(w_out, "m", None, i)))
            load_all(tiles_two())
            w.rounds(sp, NG // 2, lambda i: load_all(res_tiles(w_out2, "y2", None, i)))
            w.rounds(sp, NF, lambda i: load_all(tiles_ffn(i)))
            w.rounds(sp, NG // 2, lambda i: load_all(res_tiles(w_down, "ff", None, i, FC // 2)))
            for t in range(NT):
                sp.wait_ge(n_ready, 5 * NT + t + 1)
                sp.dma_start(out[t * P:(t + 1) * P, :], h2[:, t]).then_inc(stored, 16)
            sp.wait_ge(stored, 16 * NT)

        @block.gpsimd
        def _(pool):
            nc.gpsimd.memset(mneg_c[:, :], -0.5).then_inc(pool_c, 1)
            nc.gpsimd.memset(half_c[:, :], 0.5).then_inc(pool_c, 1)
            pool.wait_ge(pool_c, 2)

            def norm_root(k):
                c = slice(k % 2, k % 2 + 1)
                pool.wait_ge(n_mean, k + 1)
                nc.gpsimd.tensor_tensor(rstd[:, c], meansq[:, c], mneg_c[:, 0:1], ALU.pow).then_inc(n_rstd, 1)

            def spread(dst, g, s):
                pool.dma_start(dst, g.rearrange("(a n) -> a n", a=1).broadcast_to([P, D])).then_inc(s, 16)

            def lru_root(n):
                pool.wait_ge(l_nt, n + 1)
                nc.gpsimd.tensor_tensor(lt_b[:, 1], lt_b[:, 1], half_c[:, :], ALU.pow).then_inc(l_sqrt, 1)

            def ret_root(n):
                pool.wait_ge(r_var, n + 1)
                nc.gpsimd.tensor_tensor(ret_rstd, ret_var, mneg_c[:, :], ALU.pow).then_inc(r_rstd, 1)

            for k in range(2 * NT):
                norm_root(k)
            pool.wait_ge(w_used, G_X + SLOTS)
            for t in range(NT):
                pool.dma_start(x1[:, t], x[t * P:(t + 1) * P, :]).then_inc(in_res, 16)
            spread(g_row1[:, :], fin1_g, in_g1)
            for k in range(2 * NT, 3 * NT):
                norm_root(k)
            pool.wait_ge(n_ready, 3 * NT)
            for t in range(NT):
                pool.dma_start(spill[t * P:(t + 1) * P, :], x1[:, t]).then_inc(spilled, 16)
            pool.dma_start(decay[:, :, :], decay_d).then_inc(in_dec, 16)
            pool.dma_start(ga_w[:, :, :], gate_a.rearrange("n c d -> c n d")).then_inc(in_gw, 16)
            pool.dma_start(gx_w[:, :, :], gate_x.rearrange("n c d -> c n d")).then_inc(in_gw, 16)
            for k in range(3 * NT, 4 * NT):
                norm_root(k)
            for tile in tiles_two():
                if "lru" in tile:
                    lru_root(tile["lru"])
                if "ret" in tile:
                    ret_root(tile["ret"])
            pool.wait_ge(spilled, 16 * NT)
            pool.wait_ge(w_used, G_U + SLOTS)
            for t in range(NT):
                pool.dma_start(h2[:, t], spill[t * P:(t + 1) * P, :]).then_inc(in_h2, 16)
            for n in range(QUAD, 2 * QUAD):
                ret_root(n)
            for k in range(4 * NT, 5 * NT):
                norm_root(k)
            pool.wait_ge(w_used, G_U2 + SLOTS)
            spread(g_row2[:, :], fin2_g, in_g2)
            for k in range(5 * NT, 6 * NT):
                norm_root(k)

        @block.scalar
        def _(act):
            w = Walk()

            def split(tile):
                s, per = w.n["g"] % SLOTS, tile.get("per", 2)
                act.wait_ge(raw_in[s], w.slot_uses())
                act.wait_ge(w_used, w("g", 1))
                nc.scalar.activation(w_hi[:, s, 0:per], raw[:, s, 0:per], ACT.Copy).then_inc(hi_ready, 1)
                w.step("g")

            def norm(src, ready):
                for t in range(NT):
                    k = w.n["norm"]
                    ready(t)
                    if k:
                        act.wait_ge(n_mean, k)
                    nc.scalar.activation(sq_out[:, :], src[:, t], ACT.Square, accum_out=sumsq[:, k % 2:k % 2 + 1])\
                      .then_inc(n_sum, 1)
                    w.step("norm")

            def job_hi(q, hi, factors):
                pair = q % 2
                act.wait_ge(tx_done[pair], w(f"j{pair}", 1))
                for c in range(QUAD):
                    kc = q * QUAD + c
                    ins = nc.scalar.activation(hi[:, kc], bank(4 + 2 * pair, c * S, (c + 1) * S), ACT.Copy,
                                               scale=factors[:, kc:kc + 1])
                ins.then_inc(tx_hi[pair], 1)
                w.step(f"j{pair}", f"h{pair}")

            def unit_exp(unit):
                act.wait_ge(u_max, w("u", 1))
                for t in range(NT):
                    a, n = sb_at(unit, t)
                    src = scores[:, a:a + n] if unit["mask"] else ps[:, unit["s_at"][t]:unit["s_at"][t] + n]
                    ins = nc.scalar.activation(scores[:, a:a + n], src, ACT.Exp, bias=negmax[:, t:t + 1],
                                               scale=unit["scale"], accum_out=rowsum[:, t:t + 1])
                ins.then_inc(u_exp, 1)

            def unit_copy(unit):
                act.wait_ge(u_pT, w("u", 1))
                for t in range(NT):
                    a, n = sb_at(unit, t)
                    ins = nc.scalar.activation(probsT[:, a:a + n], ps[:, unit["p_at"][t]:unit["p_at"][t] + n], ACT.Copy)
                ins.then_inc(u_pTc, 1)

            def unit_hi(unit):
                act.wait_ge(u_yT, w("u", 1))
                kc, n = unit["kc"], unit["width"] // P
                nc.scalar.activation(yT_hi[:, kc:kc + n], ps[:, unit["y_at"]:unit["y_at"] + n * S].rearrange("p (c s) -> p c s", s=S),
                                     ACT.Copy, scale=0.5).then_inc(u_hi, 1)
                w.step("u")

            def ret_hi(n):
                act.wait_ge(r_yT, n + 1)
                nc.scalar.activation(y2T_hi[:, 8 + n], bank(6, 0, S), ACT.Copy, scale=gn_half[:, n:n + 1]).then_inc(r_hi, 1)

            def lru_square(n):
                if n:
                    act.wait_ge(l_y, n)
                nc.scalar.activation(gelu, lgT[:, n], ACT.Square).then_inc(l_sq, 1)

            def lru_tanh(n):
                act.wait_ge(l_arg, n + 1)
                nc.scalar.activation(gelu, gelu, ACT.Tanh, scale=float(np.sqrt(2 / np.pi)))
                act.wait_ge(l_gate, n + 1)
                nc.scalar.activation(lru_t, bank(7, 0, S), ACT.Tanh, scale=0.5, bias=gab_half[:, n:n + 1]).then_inc(l_own, 1)
                nc.scalar.activation(lru_i, bank(7, S, 2 * S), ACT.Tanh, scale=0.5, bias=gxb_half[:, n:n + 1])
                act.wait_ge(l_own, n + 1)
                nc.scalar.activation(lru_t, lru_t, ACT.Tanh, scale=ls4[:, n:n + 1], bias=ls4[:, n:n + 1]).then_inc(l_tanh, 1)

            def lru_hi(n):
                act.wait_ge(l_y, n + 1)
                nc.scalar.activation(y2T_hi[:, n], lru_y, ACT.Copy, scale=0.5).then_inc(l_hi, 1)

            def post(prev, done):
                if prev is None:
                    return
                kind, par = prev["post"], prev["par"]
                if kind[0] in ("take", "silu", "gate", "ffg"):
                    act.wait_ge(w_used, w("g", SLOTS - done))
                    dst = gates[:, kind[1]] if kind[0] == "gate" else ff_g if kind[0] == "ffg" else kind[1]
                    for t in range(NT):
                        if kind[0] == "take":
                            ins = nc.scalar.activation(dst[:, t], bank(2 * par + t), ACT.Copy)
                        else:
                            ins = nc.scalar.activation(dst[:, t], bank(2 * par + t), ACT.Tanh, scale=0.5)
                    ins.then_inc(acc_free[par] if kind[0] in ("take", "gate") else z_tanh, 1)
                w.count_post(prev)

            def post_job(prev):
                if prev is None:
                    return
                kind = prev["post"]
                if through_stage(kind):
                    act.wait_ge(tx_done[0], w("j0", 1))
                    src = ps[:, 4 * NW:6 * NW].rearrange("p (c s) -> p c s", s=S)
                    if split_job(kind):
                        dst = ffT_hi if kind[0] == "ffu" else mrgT_hi
                        nc.scalar.activation(dst[:, bass.ds(kind[-1] * QUAD, QUAD)], src, ACT.Copy, scale=0.5).then_inc(tx_hi[0], 1)
                    else:
                        nc.scalar.activation(kind[1][:, kind[2]:kind[2] + QUAD], src, ACT.Copy).then_inc(tx_free[0], 1)
                w.count_job(prev)

            def run(tile, prev, hooks=()):
                unit = tile.get("unit")
                for h in range(tile.get("hcs", HCS)):
                    split(tile)
                    if "lru" in tile and h == 1:
                        lru_square(tile["lru"])
                    if h == pos(tile, 3):
                        post(prev, h + 1)
                    if unit and h == pos(tile, 4):
                        unit_exp(unit)
                    if unit and h == pos(tile, 5):
                        unit_copy(unit)
                    if "lru" in tile and h == 5:
                        lru_tanh(tile["lru"])
                    if h == pos(tile, 6):
                        post_job(prev)
                    for f in dict(hooks).get(h, ()):
                        f()
                if unit:
                    unit_hi(unit)
                if "ret" in tile:
                    ret_hi(tile["ret"])
                if "lru" in tile:
                    lru_hi(tile["lru"])
                return tile

            def chain(tiles, prev):
                for n, tile in enumerate(tiles):
                    tile["par"] = n % 2
                    prev = run(tile, prev, tile.get("act_hooks", ()))
                return prev

            norm(mem_tok, lambda t: act.wait_ge(in_mem[t], 16))
            def jobs(hi, v, *quads):
                return [lambda q=q: job_hi(q, hi, cols[:, v:v + KC]) for q in quads]

            four = tiles_memkv()
            four[0]["act_hooks"] = {0: [lambda: act.wait_ge(cols_ready, 1)] + jobs(memT_hi, V_MEM, 0, 1),
                                    1: jobs(memT_hi, V_MEM, 2), 2: jobs(memT_hi, V_MEM, 3)}
            four[1]["act_hooks"] = {7: [lambda: norm(x_tok, lambda t: act.wait_ge(in_x[t], 16))]}
            for n in (2, 3):
                four[n]["act_hooks"] = {6: jobs(xT_hi, V_IN, 2 * n - 4), 7: jobs(xT_hi, V_IN, 2 * n - 3)}

            def log_sigmoid_exp():
                nc.scalar.activation(lamb[:, 0], lam, ACT.Abs).then_inc(lam_abs, 1)
                act.wait_ge(lam_abs, 1)
                nc.scalar.activation(lamb[:, 1], lamb[:, 0], ACT.Exp, scale=-1.0).then_inc(lam_e, 1)

            four[3]["act_hooks"][5] = [log_sigmoid_exp]
            prev = chain(four, None)
            prev = chain(tiles_attention(), prev)
            prev = chain(tiles_merge(0, first=True), prev)
            w.rounds(act, NG - 1, lambda i: chain(tiles_merge(i + 1), merge_last(i)))
            prev = merge_last(NG - 1)
            for k in range(NG // 2):
                prev = chain(res_tiles(w_out, "m", x1, k), prev)
            tiles = tiles_two()
            tiles[0]["act_hooks"] = {3: [
                lambda: norm(x1, lambda t: act.wait_ge(x_added, 1)),
                lambda: norm(x1, lambda t: act.wait_ge(n_ready, 2 * NT + t + 1)),
                *jobs(uT_hi, V_LN1, 0, 1, 2, 3)]}
            prev = chain(tiles, None)
            head, *rest = res_tiles(w_out2, "y2", h2, 0)
            head["act_hooks"] = {6: [lambda: ret_hi(4)], 7: [lambda: ret_hi(5), lambda: ret_hi(6), lambda: ret_hi(7)]}
            prev = chain([head] + rest, prev)
            prev = chain(res_tiles(w_out2, "y2", h2, 1), prev)
            tiles = tiles_ffn(0)
            tiles[0]["act_hooks"] = {3: [
                lambda: norm(h2, lambda t: act.wait_ge(x_added, 2)),
                *jobs(u2T_hi, V_LN2, 0, 1, 2, 3)]}
            chain(tiles, None)
            w.rounds(act, NF - 1, lambda i: chain(tiles_ffn(i + 1), ffn_last(i)))
            prev = ffn_last(NF - 1)
            prev = chain(res_tiles(w_down, "ff", h2, 0, FC // 2), prev)
            prev = chain(res_tiles(w_down, "ff", h2, 1, FC // 2), prev)
            norm(h2, lambda t: act.wait_ge(x_added, 3))

        @block.vector
        def _(dve):
            w = Walk()
            dve.sem_inc(lo_ready, SLOTS)

            def link(ins):
                ins.then_inc(dve_link, 1)
                w.step("link")
                dve.wait_ge(dve_link, w("link"))

            def split(tile):
                s, per = w.n["g"] % SLOTS, tile.get("per", 2)
                dve.wait_ge(hi_ready, w("g", 1))
                nc.vector.tensor_tensor(w_lo[:, s, 0:per], raw[:, s, 0:per], w_hi[:, s, 0:per].bitcast(F32), ALU.subtract)\
                  .then_inc(lo_ready, 1)
                w.step("g")

            def norm(src, dst, row=None, ready=None):
                first = w.n["norm"]
                for k in range(first, first + NT):
                    c = slice(k % 2, k % 2 + 1)
                    dve.wait_ge(n_sum, k + 1)
                    nc.vector.tensor_scalar(meansq[:, c], sumsq[:, c], 1.0 / D, EPS, ALU.mult, ALU.add).then_inc(n_mean, 1)
                    w.step("norm")
                if ready:
                    ready()
                for t in range(NT):
                    c = slice((first + t) % 2, (first + t) % 2 + 1)
                    dve.wait_ge(n_rstd, first + t + 1)
                    if row is None:
                        ins = nc.vector.tensor_scalar(dst[:, t], src[:, t], rstd[:, c], None, ALU.mult)
                    else:
                        ins = nc.vector.scalar_tensor_tensor(dst[:, t], src[:, t], rstd[:, c], row, ALU.mult, ALU.mult)
                    ins.then_inc(n_ready, 1)

            def job_lo(q, hi, lo, factors):
                pair = q % 2
                dve.wait_ge(tx_hi[pair], w(f"h{pair}", 1))
                for c in range(QUAD):
                    kc = q * QUAD + c
                    ins = nc.vector.scalar_tensor_tensor(lo[:, kc], bank(4 + 2 * pair, c * S, (c + 1) * S), factors[:, kc:kc + 1],
                                                         hi[:, kc].bitcast(F32), ALU.mult, ALU.subtract)
                ins.then_inc(tx_free[pair], 1)
                w.step(f"j{pair}", f"h{pair}")

            def unit_mask(unit):
                dve.wait_ge(u_score, w("u", 1))
                for t in range(NT):
                    a, n = sb_at(unit, t)
                    src = ps[:, unit["s_at"][t]:unit["s_at"][t] + n]
                    if unit["mask"]:
                        link(nc.vector.tensor_tensor(scores[:, a:a + n].rearrange("p (m c) -> p m c", c=P),
                                                     src.rearrange("p (m c) -> p m c", c=P), masks(unit, t), ALU.add))
                        src = scores[:, a:a + n]
                    last = nc.vector.reduce_max(rowmax[:, t:t + 1], src, AX)
                link(last)
                nc.vector.tensor_scalar(negmax, rowmax, -unit["scale"], None, ALU.mult).then_inc(u_max, 1)

            def unit_norm(unit):
                dve.wait_ge(u_exp, w("u", 1))
                link(nc.vector.reciprocal(rinv, rowsum))
                dve.wait_ge(u_out, w("u", 1))
                n = unit["width"]
                for t in range(NT):
                    ins = nc.vector.scalar_tensor_tensor(
                        y_tok[:, t, 0:n], ps[:, unit["o_at"] + t * n:unit["o_at"] + (t + 1) * n], rinv[:, t:t + 1],
                        unit["z"](t), ALU.mult, ALU.mult)
                ins.then_inc(u_y, 1)

            def unit_lo(unit):
                dve.wait_ge(u_hi, w("u", 1))
                kc, n = unit["kc"], unit["width"] // P
                nc.vector.scalar_tensor_tensor(
                    yT_lo[:, kc:kc + n], ps[:, unit["y_at"]:unit["y_at"] + n * S].rearrange("p (c s) -> p c s", s=S), 0.5,
                    yT_hi[:, kc:kc + n].bitcast(F32), ALU.mult, ALU.subtract).then_inc(u_lo, 1)
                w.step("u")

            def ret_decay(n):
                dve.wait_ge(r_score, n + 1)
                if n == 0:
                    dve.wait_ge(in_dec, 16)
                nc.vector.tensor_tensor(probsT[:, 0:S], bank(6, 0, S), decay[:, n], ALU.mult)
                nc.vector.tensor_tensor(probsT[:, S:S + P], bank(6, S, S + P), decay[:, n, 0:P], ALU.mult).then_inc(r_dec, 1)

            def ret_norm(n):
                dve.wait_ge(r_out, n + 1)
                for t in range(NT):
                    ins = nc.vector.bn_stats(stats[:, t], bank(7, t * HD, (t + 1) * HD))
                link(ins)
                for t in range(NT):
                    ins = nc.vector.bn_aggr(moments[:, t], stats[:, t])
                link(ins)
                nc.vector.tensor_scalar(ret_var, moments[:, :, 1], EPS, None, ALU.add).then_inc(r_var, 1)
                dve.wait_ge(r_rstd, n + 1)
                for t in range(NT):
                    ins = nc.vector.tensor_scalar(y_tok[:, t, 0:HD], bank(7, t * HD, (t + 1) * HD), moments[:, t, 0:1],
                                                  ret_rstd[:, t:t + 1], ALU.subtract, ALU.mult)
                link(ins)
                half, h = n // QUAD, n % QUAD
                nc.vector.tensor_tensor(y_tok[:, :, 0:HD], y_tok[:, :, 0:HD], gr[half][:, :, h * HD:(h + 1) * HD], ALU.mult)\
                  .then_inc(r_y, 1)

            def ret_lo(n):
                dve.wait_ge(r_hi, n + 1)
                nc.vector.scalar_tensor_tensor(y2T_lo[:, 8 + n], bank(6, 0, S), gn_half[:, n:n + 1],
                                               y2T_hi[:, 8 + n].bitcast(F32), ALU.mult, ALU.subtract).then_inc(r_lo, 1)

            def lru_conv(n):
                xin = lxT[:, n]
                tap = lambda k: cols[:, V_CONVW + 8 * k + n:V_CONVW + 8 * k + n + 1]
                dve.wait_ge(l_sq, n + 1)
                link(nc.vector.tensor_scalar(gelu, gelu, 0.044715, 1.0, ALU.mult, ALU.add))
                nc.vector.tensor_tensor(gelu, gelu, lgT[:, n], ALU.mult).then_inc(l_arg, 1)
                link(nc.vector.tensor_scalar(lru_u, xin, tap(3), cols[:, V_CONVB + n:V_CONVB + n + 1], ALU.mult, ALU.add))
                for d in (1, 2, 3):
                    ins = nc.vector.scalar_tensor_tensor(lru_u[:, d:S], xin[:, 0:S - d], tap(3 - d), lru_u[:, d:S], ALU.mult, ALU.add)
                    if d < 3:
                        link(ins)
                ins.then_inc(l_conv, 1)

            def lru_decay(n):
                dve.wait_ge(l_tanh, n + 1)
                nc.vector.tensor_scalar(lru_root_, lru_t, -1.0, 1e-30, ALU.mult, ALU.max).then_inc(l_nt, 1)
                link(nc.vector.tensor_scalar(lru_r, lru_t, -1.0, 1.0, ALU.mult, ALU.add))
                link(nc.vector.reciprocal(lru_r, lru_r))
                nc.vector.scalar_tensor_tensor(lru_a, lru_t, 1.0, lru_r, ALU.add, ALU.mult)
                link(nc.vector.scalar_tensor_tensor(lru_i, lru_i, 1.0, lru_u, ALU.add, ALU.mult))
                link(nc.vector.tensor_tensor(lru_i, lru_i, lru_r, ALU.mult))
                link(nc.vector.scalar_tensor_tensor(lru_y, gelu, 1.0, lgT[:, n], ALU.add, ALU.mult))

            def lru_scan(n):
                dve.wait_ge(l_sqrt, n + 1)
                link(nc.vector.tensor_tensor(lru_i, lru_i, lru_root_, ALU.mult))
                link(nc.vector.tensor_tensor_scan(lru_r, lru_a, lru_i, 0.0, ALU.mult, ALU.add))
                nc.vector.tensor_tensor(lru_y, lru_y, lru_r, ALU.mult).then_inc(l_y, 1)

            def lru_lo(n):
                dve.wait_ge(l_hi, n + 1)
                nc.vector.scalar_tensor_tensor(y2T_lo[:, n], lru_y, 0.5, y2T_hi[:, n].bitcast(F32),
                                               ALU.mult, ALU.subtract).then_inc(l_lo, 1)

            def rotate(par):
                for t in range(NT):
                    cos = consts[:, C_COS + t * 64:C_COS + (t + 1) * 64]
                    sin = consts[:, C_SIN + t * 128:C_SIN + (t + 1) * 128].rearrange("p (a d) -> p a d", a=2)
                    acc = bank(2 * par + t)
                    nc.vector.tensor_tensor(stage[:, t].rearrange("p (a d) -> p a d", d=64), acc.rearrange("p (a d) -> p a d", d=64),
                                            cos[:, None, :].broadcast_to([P, 2 * QUAD, 64]), ALU.mult)
                    a4 = acc.rearrange("p (h a d) -> p h a d", a=2, d=64)
                    t4 = tmp[:, t].rearrange("p (h a d) -> p h a d", a=2, d=64)
                    for a in range(2):
                        last = nc.vector.tensor_tensor(t4[:, :, a], a4[:, :, 1 - a],
                                                       sin[:, a][:, None, :].broadcast_to([P, QUAD, 64]), ALU.mult)
                link(last)
                nc.vector.tensor_tensor(stage[:, :, :], stage[:, :, :], tmp[:, :, :], ALU.add).then_inc(st_ready, 1)

            def post(prev, done, signal=None):
                if prev is None:
                    return
                kind, par = prev["post"], prev["par"]
                accs = [bank(2 * par + t) for t in range(NT)]
                if kind[0] in ("silu", "ffg"):
                    dst = kind[1] if kind[0] == "silu" else ff_g
                    dve.wait_ge(z_tanh, w("z", 1))
                    for t in range(NT):
                        last = nc.vector.scalar_tensor_tensor(dst[:, t], dst[:, t], 1.0, accs[t], ALU.add, ALU.mult)
                    last.then_inc(acc_free[par], 1)
                elif kind[0] not in ("take", "gate"):
                    dve.wait_ge(w_used, w("g", SLOTS - done))
                if through_stage(kind) or kind[0] == "mix" and kind[2] == "first":
                    if w.n["j0"]:
                        dve.wait_ge(tx_done[0], w("j0"))
                if kind[0] == "turn":
                    for t in range(NT):
                        last = nc.vector.tensor_copy(stage[:, t], accs[t])
                    last.then_inc(st_ready, 1)
                if kind[0] == "rope":
                    rotate(par)
                if kind[0] == "mix":
                    gate = gates[:, kind[1]]
                    to = stage if kind[2] == "first" else tmp
                    for t in range(NT):
                        last = nc.vector.scalar_tensor_tensor(to[:, t], gate[:, t], 1.0, accs[t], ALU.add, ALU.mult)
                    if kind[2] == "last":
                        link(last)
                        nc.vector.tensor_tensor(stage[:, :, :], stage[:, :, :], tmp[:, :, :], ALU.add).then_inc(st_ready, 1)
                    else:
                        last.then_inc(acc_free[par], 1)
                        dve.wait_ge(acc_free[par], w(f"a{par}", 1))
                        if kind[2] == "more":
                            link(nc.vector.tensor_tensor(stage[:, :, :], stage[:, :, :], tmp[:, :, :], ALU.add))
                if kind[0] == "ffu":
                    for t in range(NT):
                        last = nc.vector.tensor_tensor(stage[:, t], ff_g[:, t], accs[t], ALU.mult)
                    last.then_inc(st_ready, 1)
                if kind[0] == "res":
                    for t in range(NT):
                        c = kind[1][:, t, bass.ds(kind[2] * NW, NW)]
                        last = nc.vector.tensor_tensor(c, c, accs[t], ALU.add)
                    last.then_inc(signal or acc_free[par], 1)
                if signal is None:
                    w.count_post(prev)

            def post_job(prev):
                if prev is None:
                    return
                kind = prev["post"]
                if through_stage(kind) and split_job(kind):
                    hi, lo = (ffT_hi, ffT_lo) if kind[0] == "ffu" else (mrgT_hi, mrgT_lo)
                    c = bass.ds(kind[-1] * QUAD, QUAD)
                    dve.wait_ge(tx_hi[0], w("h0", 1))
                    nc.vector.scalar_tensor_tensor(lo[:, c], ps[:, 4 * NW:6 * NW].rearrange("p (c s) -> p c s", s=S), 0.5,
                                                   hi[:, c].bitcast(F32), ALU.mult, ALU.subtract).then_inc(tx_free[0], 1)
                w.count_job(prev)

            def run(tile, prev, hooks=()):
                unit = tile.get("unit")
                for h in range(tile.get("hcs", HCS)):
                    split(tile)
                    if "lru" in tile and h == 2:
                        lru_conv(tile["lru"])
                    if h == pos(tile, 3):
                        post(prev, h + 1)
                    if unit and h == pos(tile, 4):
                        unit_mask(unit)
                    if "ret" in tile and h == 4:
                        ret_decay(tile["ret"])
                    if "lru" in tile and h == 6:
                        lru_decay(tile["lru"])
                    if h == pos(tile, 6):
                        post_job(prev)
                    for f in dict(hooks).get(h, ()):
                        f()
                if unit:
                    unit_norm(unit)
                    unit_lo(unit)
                if "ret" in tile:
                    ret_norm(tile["ret"])
                if "lru" in tile:
                    lru_scan(tile["lru"])
                if "ret" in tile:
                    ret_lo(tile["ret"])
                if "lru" in tile:
                    lru_lo(tile["lru"])
                return tile

            def chain(tiles, prev):
                for n, tile in enumerate(tiles):
                    tile["par"] = n % 2
                    prev = run(tile, prev, tile.get("dve_hooks", ()))
                return prev

            def log_sigmoid():
                dve.wait_ge(lam_e, 1)
                e, den, s_, s2, acc = (lamb[:, k] for k in (1, 2, 3, 4, 5))
                link(nc.vector.tensor_scalar(den, e, 2.0, None, ALU.add))
                link(nc.vector.reciprocal(den, den))
                link(nc.vector.tensor_tensor(s_, e, den, ALU.mult))
                link(nc.vector.tensor_tensor(s2, s_, s_, ALU.mult))
                terms = [1.0 / (2 * k + 1) for k in range(9)]
                link(nc.vector.tensor_scalar(acc, s2, terms[8], terms[7], ALU.mult, ALU.add))
                for c in terms[6::-1]:
                    link(nc.vector.tensor_tensor(acc, acc, s2, ALU.mult))
                    link(nc.vector.tensor_scalar(acc, acc, c, None, ALU.add))
                link(nc.vector.tensor_tensor(acc, acc, s_, ALU.mult))
                link(nc.vector.tensor_scalar(den, lam, 0.0, 2.0, ALU.min, ALU.mult))
                nc.vector.scalar_tensor_tensor(ls4, acc, -4.0, den, ALU.mult, ALU.add).then_inc(lam_ready, 1)

            norm(mem_tok, mem_tok)
            dve.wait_ge(vec_ps, 1)
            nc.vector.tensor_copy(cols[:, 0:V_END], bank(0, 0, V_END)).then_inc(cols_ready, 1)
            dve.wait_ge(cols_ready, 1)
            nc.vector.tensor_scalar(gn_half, cols[:, V_GN:V_GN + 8], 0.5, None, ALU.mult)
            link(nc.vector.tensor_scalar(gab_half[:, 0:16], cols[:, V_GAB:V_GAB + 16], 0.5, None, ALU.mult))
            def jobs(hi, lo, v, *quads):
                return [lambda q=q: job_lo(q, hi, lo, cols[:, v:v + KC]) for q in quads]

            four = tiles_memkv()
            four[0]["dve_hooks"] = {0: jobs(memT_hi, memT_lo, V_MEM, 0, 1), 1: jobs(memT_hi, memT_lo, V_MEM, 2),
                                    2: jobs(memT_hi, memT_lo, V_MEM, 3)}
            four[1]["dve_hooks"] = {7: [lambda: norm(x_tok, x_tok)]}
            for n in (2, 3):
                four[n]["dve_hooks"] = {6: jobs(xT_hi, xT_lo, V_IN, 2 * n - 4), 7: jobs(xT_hi, xT_lo, V_IN, 2 * n - 3)}
            prev = chain(four, None)
            log_sigmoid()
            prev = chain(tiles_attention(), prev)
            prev = chain(tiles_merge(0, first=True), prev)
            w.rounds(dve, NG - 1, lambda i: chain(tiles_merge(i + 1), merge_last(i)))
            prev = merge_last(NG - 1)
            for k in range(NG // 2):
                tiles = res_tiles(w_out, "m", x1, k)
                if k == 0:
                    tiles[1]["dve_hooks"] = {2: [lambda: dve.wait_ge(in_res, 16 * NT)]}
                prev = chain(tiles, prev)
            tiles = tiles_two()
            tiles[0]["dve_hooks"] = {3: [
                lambda: post(prev, 4, x_added),
                lambda: norm(x1, x1, g_row1[:, :], lambda: dve.wait_ge(in_g1, 16)),
                lambda: norm(x1, u_tok),
                *jobs(uT_hi, uT_lo, V_LN1, 0, 1, 2, 3)]}
            prev = chain(tiles, None)
            head, *rest = res_tiles(w_out2, "y2", h2, 0)
            rest[0]["dve_hooks"] = {2: [lambda: dve.wait_ge(in_h2, 16 * NT)]}
            head["dve_hooks"] = {
                4: [lambda: ret_decay(4)], 5: [lambda: ret_norm(4)], 6: [lambda: ret_lo(4), lambda: ret_decay(5)],
                7: [lambda: ret_norm(5), lambda: ret_lo(5)] + [f for n in (6, 7) for f in (
                    lambda n=n: ret_decay(n), lambda n=n: ret_norm(n), lambda n=n: ret_lo(n))]}
            prev = chain([head] + rest, prev)
            prev = chain(res_tiles(w_out2, "y2", h2, 1), prev)
            tiles = tiles_ffn(0)
            tiles[0]["dve_hooks"] = {3: [
                lambda: post(prev, 4, x_added),
                lambda: norm(h2, u2_tok),
                *jobs(u2T_hi, u2T_lo, V_LN2, 0, 1, 2, 3)]}
            chain(tiles, None)
            w.rounds(dve, NF - 1, lambda i: chain(tiles_ffn(i + 1), ffn_last(i)))
            prev = ffn_last(NF - 1)
            prev = chain(res_tiles(w_down, "ff", h2, 0, FC // 2), prev)
            prev = chain(res_tiles(w_down, "ff", h2, 1, FC // 2), prev)
            post(prev, 0, x_added)
            norm(h2, h2, g_row2[:, :], lambda: dve.wait_ge(in_g2, 16))

        @block.tensor
        def _(pe):
            w = Walk()
            pe.sem_inc(w_used, SLOTS)

            def transposes(src, dst, n):
                for c in range(n):
                    for t in range(NT):
                        o = dst + c * S + t * P
                        ins = nc.tensor.transpose(ps[:, o:o + P], src(t, c), ident)
                return ins

            def job(q, src, ready):
                pair = q % 2
                pe.wait_ge(n_ready, ready)
                if w.n[f"j{pair}"]:
                    pe.wait_ge(tx_free[pair], w(f"j{pair}"))
                transposes(lambda t, c: src[:, t, (q * QUAD + c) * P:(q * QUAD + c + 1) * P], (4 + 2 * pair) * NW, QUAD)\
                    .then_inc(tx_done[pair], 1)
                w.step(f"j{pair}", f"h{pair}")

            def parts_ready(q):
                pe.wait_ge(tx_free[q % 2], quads[q])

            quads = {}

            def unit_scores(unit):
                u = w.n["u"]
                if u:
                    pe.wait_ge(u_lo, u)
                pe.wait_ge(tx_free[0], w.n["j0"])
                pe.wait_ge(tx_free[1], w.n["j1"])
                for t in range(NT):
                    o = unit["s_at"][t]
                    for (qs, ks, _), kt in unit["blocks"][t]:
                        for n, ((qT, qc), (kT, kc)) in enumerate(zip(qs, ks)):
                            ins = nc.tensor.matmul(ps[:, o:o + P], qT[:, qc, t * P:(t + 1) * P], kT[:, kc, kt * P:(kt + 1) * P],
                                                   start=n == 0, stop=n == len(qs) - 1)
                        o += P
                ins.then_inc(u_score, 1)

            def unit_turn(unit):
                pe.wait_ge(u_exp, w("u", 1))
                for t in range(NT):
                    a, n = sb_at(unit, t)
                    for c in range(0, n, P):
                        o = unit["p_at"][t] + c
                        ins = nc.tensor.transpose(ps[:, o:o + P], scores[:, a + c:a + c + P], ident)
                ins.then_inc(u_pT, 1)

            def unit_values(unit):
                pe.wait_ge(u_pTc, w("u", 1))
                width = unit["width"]
                for t in range(NT):
                    a, _ = sb_at(unit, t)
                    blocks = unit["blocks"][t]
                    for n, ((_, _, v), kt) in enumerate(blocks):
                        o = unit["o_at"] + t * width
                        ins = nc.tensor.matmul(ps[:, o:o + width], probsT[:, a + n * P:a + (n + 1) * P], v(kt),
                                               start=n == 0, stop=n == len(blocks) - 1)
                ins.then_inc(u_out, 1)

            def unit_y(unit):
                pe.wait_ge(u_y, w("u", 1))
                transposes(lambda t, c: y_tok[:, t, c * P:(c + 1) * P], unit["y_at"], unit["width"] // P).then_inc(u_yT, 1)
                w.step("u")

            def ret_scores(n):
                if n:
                    pe.wait_ge(r_lo, n)
                pe.wait_ge(tx_free[0], w.n["j0"])
                pe.wait_ge(tx_free[1], w.n["j1"])
                half, h = n // QUAD, n % QUAD
                q, k = qrT[half], krT[half]
                nc.tensor.matmul(bank(6, 0, S), k[:, h, 0:P], q[:, h, 0:S], start=True, stop=True)
                nc.tensor.matmul(bank(6, S, S + P), k[:, h, P:S], q[:, h, P:S], start=True, stop=True).then_inc(r_score, 1)

            def ret_values(n):
                pe.wait_ge(r_dec, n + 1)
                if n < QUAD:
                    pe.wait_ge(l_tanh, min(n + 5, 8))
                half, h = n // QUAD, n % QUAD
                v = [vr[half][:, t, h * HD:(h + 1) * HD] for t in range(NT)]
                nc.tensor.matmul(bank(7, 0, HD), probsT[:, 0:P], v[0], start=True, stop=True)
                nc.tensor.matmul(bank(7, HD, 2 * HD), probsT[:, P:S], v[0], start=True, stop=False)
                nc.tensor.matmul(bank(7, HD, 2 * HD), probsT[:, S:S + P], v[1], start=False, stop=True).then_inc(r_out, 1)

            def ret_y(n):
                pe.wait_ge(r_y, n + 1)
                transposes(lambda t, c: y_tok[:, t, 0:HD], 6 * NW, 1).then_inc(r_yT, 1)

            def lru_gates(n, heads):
                pe.wait_ge(l_conv, n + 1)
                if n == 0:
                    pe.wait_ge(in_gw, 32)
                    pe.wait_ge(tx_free[1], w.n["j1"])
                if heads:
                    pe.wait_ge(r_y, heads)
                nc.tensor.matmul(bank(7, 0, S), ga_w[:, n], lru_u, start=True, stop=True)
                nc.tensor.matmul(bank(7, S, 2 * S), gx_w[:, n], lru_u, start=True, stop=True).then_inc(l_gate, 1)

            def post(prev):
                if prev is None:
                    return
                w.count_post(prev)
                if through_stage(prev["post"]):
                    pe.wait_ge(st_ready, w("st", 1))
                    if w.n["j0"]:
                        pe.wait_ge(tx_free[0], w("j0"))
                    transposes(lambda t, c: stage[:, t, c * P:(c + 1) * P], 4 * NW, QUAD).then_inc(tx_done[0], 1)
                w.count_job(prev)

            def run(tile, prev):
                par, hcs, per, k0 = tile["par"], tile.get("hcs", HCS), tile.get("per", 2), tile.get("k0", 0)
                hi, lo = PARTS[tile["x"]]
                unit, need, hooks = tile.get("unit"), tile.get("need", {}), tile.get("pe_hooks", {})
                if w.n[f"a{par}"]:
                    pe.wait_ge(acc_free[par], w(f"a{par}"))
                at_ = (0, 1, 2, 3) if hcs == 4 else (0, 2, 4, 5)
                for h in range(hcs):
                    s = w.n["g"] % SLOTS
                    for f in need.get(h, ()):
                        f()
                    pe.wait_ge(lo_ready, w("g", SLOTS + 1))
                    for k in range(per):
                        kc = h * per + k
                        first, last = kc == 0, kc == hcs * per - 1
                        for t in range(NT):
                            x_hi, x_lo = (m[:, k0 + kc, t * P:(t + 1) * P] for m in (hi, lo))
                            nc.tensor.matmul(bank(2 * par + t), x_hi, w_hi[:, s, k], start=first, stop=False)
                            nc.tensor.matmul(bank(2 * par + t), x_hi, w_lo[:, s, k], start=False, stop=False)
                            ins = nc.tensor.matmul(bank(2 * par + t), x_lo, w_hi[:, s, k], start=False, stop=last)
                    ins.then_inc(w_used, 1)
                    w.step("g")
                    if unit and h in at_:
                        (unit_scores, unit_turn, unit_values, unit_y)[at_.index(h)](unit)
                    if "ret" in tile and h == 0:
                        ret_scores(tile["ret"])
                    if "lru" in tile and h == 1:
                        lru_gates(tile["lru"], tile.get("ret", 0))
                    if h == pos(tile, 3):
                        post(prev)
                    if "ret" in tile and h == 5:
                        ret_values(tile["ret"])
                    if "ret" in tile and h == 6:
                        ret_y(tile["ret"])
                    for f in hooks.get(h, ()):
                        f()
                return tile

            def chain(tiles, prev):
                for n, tile in enumerate(tiles):
                    tile["par"] = n % 2
                    prev = run(tile, prev)
                return prev

            def begin(tile, src, ready):
                for q in range(QUAD):
                    quads[q] = w.n[f"j{q % 2}"] + q // 2 + 1
                for q in range(2):
                    job(q, src, ready)
                tile["pe_hooks"] = {0: [lambda: job(2, src, ready)], 1: [lambda: job(3, src, ready)]}
                tile["need"] = {2 * q: [lambda q=q: parts_ready(q)] for q in range(QUAD)}

            pe.wait_ge(in_const, 16)
            pe.wait_ge(in_vec, 32)
            nc.tensor.transpose(bank(0, 0, P), vec_a[:, :], ident)
            nc.tensor.transpose(bank(0, P, V_END), vec_b[0:V_END - P, :], ident[0:V_END - P, 0:V_END - P]).then_inc(vec_ps, 1)
            four = tiles_memkv()
            begin(four[0], mem_tok, NT)
            four[0]["need"][0].append(lambda: pe.wait_ge(cols_ready, 1))
            for n in (2, 3):
                four[n]["pe_hooks"] = {k: [lambda q=q: job(q, x_tok, 2 * NT)] for k, q in ((4, 2 * (n - 2)), (5, 2 * (n - 2) + 1))}
            prev = chain(four, None)
            tiles = tiles_attention()
            tiles[0]["need"] = {0: [lambda: pe.wait_ge(tx_free[0], w.n["j0"]), lambda: pe.wait_ge(tx_free[1], w.n["j1"])]}
            prev = chain(tiles, prev)
            tiles = tiles_merge(0, first=True)
            for k, units in ((3, 4), (4, 12), (5, 16)):
                tiles[k]["need"] = {0: [lambda units=units: pe.wait_ge(u_lo, units)]}
            prev = chain(tiles, prev)
            w.rounds(pe, NG - 1, lambda i: chain(tiles_merge(i + 1), merge_last(i)))
            prev = merge_last(NG - 1)
            for k in range(NG // 2):
                tiles = res_tiles(w_out, "m", x1, k)
                if k == 0:
                    tiles[0]["need"] = {0: [lambda: pe.wait_ge(tx_free[0], w.n["j0"])],
                                        6: [lambda: pe.wait_ge(tx_free[0], w.n["j0"])]}
                prev = chain(tiles, prev)
            tiles = tiles_two()
            begin(tiles[0], u_tok, 4 * NT)
            prev = chain(tiles, None)
            head, *rest = res_tiles(w_out2, "y2", h2, 0)
            head["need"] = {0: [lambda: pe.wait_ge(l_lo, 8)], 4: [lambda: pe.wait_ge(r_lo, 4)],
                            6: [lambda: pe.wait_ge(r_lo, 6)], 7: [lambda: pe.wait_ge(r_lo, 8)]}
            head["pe_hooks"] = {
                0: [lambda: ret_scores(4)], 1: [lambda: ret_values(4)], 2: [lambda: ret_y(4), lambda: ret_scores(5)],
                3: [lambda: ret_values(5)], 4: [lambda: ret_y(5), lambda: ret_scores(6)], 5: [lambda: ret_values(6)],
                6: [lambda: ret_y(6), lambda: ret_scores(7), lambda: ret_values(7), lambda: ret_y(7)]}
            prev = chain([head] + rest, prev)
            prev = chain(res_tiles(w_out2, "y2", h2, 1), prev)
            tiles = tiles_ffn(0)
            begin(tiles[0], u2_tok, 5 * NT)
            chain(tiles, None)
            w.rounds(pe, NF - 1, lambda i: chain(tiles_ffn(i + 1), ffn_last(i)))
            prev = ffn_last(NF - 1)
            for k in range(NG // 2):
                tiles = res_tiles(w_down, "ff", h2, k, FC // 2)
                if k == 0:
                    tiles[0]["need"] = {0: [lambda: pe.wait_ge(tx_free[0], w.n["j0"])],
                                        FC // 2 - 2: [lambda: pe.wait_ge(tx_free[0], w.n["j0"])]}
                prev = chain(tiles, prev)


def shape_tables():
    f32 = np.float32
    half = HD // 2
    freq = (f32(10000.0) ** (-np.arange(half, dtype=f32) / f32(half))).astype(f32)
    angle = (np.arange(S, dtype=f32)[:, None] * freq[None, :]).astype(f32).astype(np.float64)
    cos, sin = np.cos(angle), np.sin(angle)
    c = np.zeros((P, C_END), f32)
    c[:, C_ID:C_ID + P] = np.eye(P)
    row, col = np.arange(P)[:, None], np.arange(P)[None, :]
    for t in range(NT):
        c[:, C_COS + t * half:C_COS + (t + 1) * half] = cos[t * P:(t + 1) * P]
        c[:, C_SIN + t * HD:C_SIN + t * HD + half] = -sin[t * P:(t + 1) * P]
        c[:, C_SIN + t * HD + half:C_SIN + (t + 1) * HD] = sin[t * P:(t + 1) * P]
    causal = col <= row
    same = [(row - col) % d == 0 for d in (4, 16)]
    seen = [np.ones((P, P), bool), causal, col >= row, causal,
            same[0], causal & same[0], same[1], causal & same[1]]
    for m, ok in enumerate(seen):
        c[:, C_MASK + m * P:C_MASK + (m + 1) * P] = np.where(ok, 0.0, -1e30)
    log_gamma = np.log1p(-np.exp2(-5.0 - np.arange(8)))
    ahead = np.arange(S)[None, :] - np.arange(P)[:, None]
    decay = np.where(ahead >= 0, np.exp(log_gamma[:, None, None] * np.maximum(ahead, 0)), 0.0) * HD ** -0.5
    return c, np.ascontiguousarray(decay.transpose(1, 0, 2)).astype(f32)


_IN = ("x", "mem", "w_in", "w_mem_kv", "w_proj_a", "w_proj_b", "w_proj_m", "w_out", "norm_final_g", "w_in_2", "w_out_2",
       "w_ffn_gate_2", "w_ffn_up_2", "w_ffn_down_2", "final_norm_w_2", "gate_a_w_2", "gate_x_w_2")
_VEC = ("norm_mem_g", "norm_in_g", "ln1_w_2", "ln2_w_2", "ret_gn_w_2", "conv_w_2", "conv_b_2", "gate_a_b_2", "gate_x_b_2",
        "lru_lambda_2")


def kernel(**inputs):
    import concourse.bacc as bacc
    from concourse.bass_utils import run_bass_kernel_spmd

    nc = bacc.Bacc("TRN2", target_bir_lowering=False, num_devices=1)
    arrays, args = {}, []

    def give(name, a):
        arrays[name] = a
        args.append(nc.dram_tensor(name, a.shape, mybir.dt.from_np(a.dtype), kind="ExternalInput").ap())

    for name in _IN:
        a = np.ascontiguousarray(inputs[name])
        while a.ndim > 1 and a.shape[0] == 1:
            a = a[0]
        give(f"in_{name}", a)
    give("in_vectors", np.concatenate([np.asarray(inputs[name]).reshape(-1, P) for name in _VEC]))
    consts, decay = shape_tables()
    give("in_consts", consts)
    give("in_decay", decay)
    args.append(nc.dram_tensor("h_spill", (S, D), F32, kind="Internal").ap())
    args.append(nc.dram_tensor("out_dram", (S, D), F32, kind="ExternalOutput").ap())
    build(nc, *args)
    r = run_bass_kernel_spmd(nc, [arrays], core_ids=[0])
    return r.results[0]["out_dram"].reshape(1, S, D)
```

```python
from contextlib import ExitStack

import numpy as np

import concourse.bass as bass
from concourse import mybir

ALU = mybir.AluOpType
ACT = mybir.ActivationFunctionType
F32 = mybir.dt.float32
F32R = mybir.dt.float32r
BF16 = mybir.dt.bfloat16
AX = mybir.AxisListType.X

P = 128
S = 256
NT = S // P
D = 2048
KC = D // P
NW = 512
HD = 128
EPS = 1e-6
SLOTS = 4
KIB = 1024
SBUF0 = 16640
QUAD = NW // HD

C_ID, C_COS, C_SIN, C_MASK = 0, 128, 256, 512
C_END = C_MASK + 8 * P
M_NONE, M_CAUSAL, M_DIL = 0, 1, 2

V_MEM, V_IN, V_LN1, V_LN2, V_GN, V_CONVW, V_CONVB, V_GAB, V_GXB, V_LAM, V_END = (
    0, 16, 32, 48, 64, 72, 104, 112, 120, 128, 136)


class Walk:

    NAMES = ("g", "a0", "a1", "z", "st", "j0", "j1", "h0", "h1", "sq", "u", "link")

    def __init__(self):
        self.n = dict.fromkeys(self.NAMES, 0)
        self.loop = None

    def __call__(self, name, plus=0):
        if self.loop is None or not self.loop[1][name]:
            return self.n[name] + plus
        i, per = self.loop
        return i * per[name] + (self.n[name] + plus)

    def slot_uses(self):
        uses = 16 * (self.n["g"] // SLOTS + 1)
        return uses if self.loop is None else self.loop[0] * (16 * self.loop[1]["g"] // SLOTS) + uses

    def step(self, *names):
        for name in names:
            self.n[name] += 1

    def rounds(self, eng, count, body):
        before = dict(self.n)
        body(0)
        per = {k: self.n[k] - before[k] for k in self.n}
        assert per["g"] % SLOTS == 0
        if count > 1:
            self.n = dict(before)
            with eng.Fori(1, count) as i:
                self.loop = (i, per)
                body(i)
            self.loop = None
        self.n = {k: before[k] + count * per[k] for k in before}

    def count_post(self, prev):
        kind = prev["post"]
        if not through_stage(kind):
            self.step(f"a{prev['par']}")
        if kind[0] in ("silu", "ffg"):
            self.step("z")

    def count_job(self, prev):
        if through_stage(prev["post"]):
            self.step("st", "j0", *(("h0",) if split_job(prev["post"]) else ()))


def through_stage(kind):
    return kind[0] in ("turn", "rope", "ffu") or kind[0] == "res" and kind[3] != "out" or kind[0] == "mix" and kind[2] == "last"


def split_job(kind):
    return kind[0] in ("ffu", "mix", "res")


def build(nc, x, mem, w_in, w_mkv, w_pa, w_pb, w_pm, w_out, fin1_g, w_in2, w_out2, w_gate, w_up, w_down,
          fin2_g, gate_a, gate_x, vecs, consts_d, decay_d, spill, out):
    ctx = ExitStack()
    with ctx:
        def at(name, shape, dt, kib):
            return nc.alloc_sbuf_tensor_at(name, shape, dt, offset=SBUF0 + int(kib * KIB))

        def sem(name):
            return ctx.enter_context(nc.semaphore(name))

        raw = at("raw", [P, SLOTS, 2, NW], F32, 0)
        w_hi = at("w_hi", [P, SLOTS, 2, NW], F32R, 16)
        w_lo = at("w_lo", [P, SLOTS, 2, NW], F32R, 32)
        xT_hi = at("xT_hi", [P, KC, S], F32R, 48)
        xT_lo = at("xT_lo", [P, KC, S], F32R, 64)
        memT_hi = at("memT_hi", [P, KC, S], F32R, 80)
        memT_lo = at("memT_lo", [P, KC, S], F32R, 96)
        yT_hi = at("yT_hi", [P, 20, S], F32R, 80)
        yT_lo = at("yT_lo", [P, 20, S], F32R, 100)
        x_tok = at("x_tok", [P, NT, D], F32, 120)
        mem_tok = at("mem_tok", [P, NT, D], F32, 136)
        qmT = at("qmT", [P, 8, S], F32, 136)
        zm = at("zm", [P, NT, 1024], F32, 144)
        mv = at("mv", [P, NT, 1024], F32, 152)
        mkT = at("mkT", [P, 8, S], F32, 160)
        half_at = (120, 160)
        qaT, kaT, va, za = (
            [at(f"{n}{h}", s, F32, half_at[h] + 4 * m) for h in range(2)]
            for m, (n, s) in enumerate((("qaT", [P, QUAD, S]), ("kaT", [P, QUAD, S]), ("va", [P, NT, NW]), ("za", [P, NT, NW]))))
        qbT = at("qbT", [P, 12, S], F32, 120)
        kbT = at("kbT", [P, 12, S], F32, 132)
        vb = at("vb", [P, 3, NT, NW], F32, 144)
        zb = at("zb", [P, NT, NW], F32, 156)
        gates = at("gates", [P, 3, NT, NW], F32, 160)
        mrgT_hi = at("mrgT_hi", [P, KC, S], F32R, 120)
        mrgT_lo = at("mrgT_lo", [P, KC, S], F32R, 136)
        x1 = at("x1", [P, NT, D], F32, 48)
        uT_hi = at("uT_hi", [P, KC, S], F32R, 80)
        uT_lo = at("uT_lo", [P, KC, S], F32R, 96)
        lxT = at("lxT", [P, 8, S], F32, 64)
        lgT = at("lgT", [P, 8, S], F32, 72)
        decay = at("decay", [P, 8, S], F32, 112)
        ret_at = (120, 136)
        qrT, krT, vr, gr = (
            [at(f"{n}{h}", s, F32, ret_at[h] + 4 * m) for h in range(2)]
            for m, (n, s) in enumerate((("qrT", [P, QUAD, S]), ("krT", [P, QUAD, S]), ("vr", [P, NT, NW]), ("gr", [P, NT, NW]))))
        ga_w = at("ga_w", [P, 8, P], F32, 152)
        gx_w = at("gx_w", [P, 8, P], F32, 156)
        y2T_hi = at("y2T_hi", [P, KC, S], F32R, 48)
        y2T_lo = at("y2T_lo", [P, KC, S], F32R, 160)
        h2 = at("h2", [P, NT, D], F32, 92)
        u2T_hi = at("u2T_hi", [P, KC, S], F32R, 108)
        u2T_lo = at("u2T_lo", [P, KC, S], F32R, 124)
        FC = w_down.shape[0] // P
        ffT_lo = at("ffT_lo", [P, FC, S], F32R, 48)
        ffT_hi = at("ffT_hi", [P, FC, S], F32R, 140)
        g_row1 = at("g_row1", [P, D], F32, 176)
        g_row2 = at("g_row2", [P, D], F32, 108)
        scores = at("scores", [P, 1152], F32, 176)
        probsT = at("probsT", [P, 1152], F32, 180.5)
        consts = at("consts", [P, C_END], F32, 185)
        ident = consts[:, C_ID:C_ID + P]
        lt_a = at("lt_a", [P, 4, S], F32, 176)
        lt_b = at("lt_b", [P, 4, S], F32, 187)
        lru_u, lru_t, lru_i, lru_r = (lt_a[:, k] for k in range(4))
        lru_a, lru_root, lru_y, gelu = (lt_b[:, k] for k in range(4))
        stage = at("stage", [P, NT, NW], F32, 191)
        tmp = at("tmp", [P, NT, NW], F32, 195)
        sq_out = at("sq_out", [P, D], BF16, 195)
        y_tok = at("y_tok", [P, NT, S], F32, 199)
        ff_g = at("ff_g", [P, NT, NW], F32, 186)
        cols = at("cols", [P, V_END], F32, 201)
        vec_a = at("vec_a", [P, P], F32, 202)
        vec_b = at("vec_b", [P, P], F32, 202.5)
        small = at("small", [P, 128], F32, 203)
        rot = at("rot", [P, NT, 192], F32, 205)
        lamb = at("lamb", [P, 8, 8], F32, 203.5)
        mneg_c = at("mneg_c", [P, 2], F32, 204.75)

        rowmax, negmax, rowsum, rinv = (small[:, k:k + 2] for k in (0, 2, 4, 6))
        sumsq_m, sumsq_x, meansq, r_first, sum_ab = (small[:, k:k + 2] for k in (8, 10, 12, 14, 36))
        stats = small[:, 16:28].rearrange("p (t s) -> p t s", t=2)
        moments = small[:, 28:32].rearrange("p (t s) -> p t s", t=2)
        ret_rstd = small[:, 32:34]
        ret_var = small[:, 34:36]
        gn_half = small[:, 40:48]
        gab_half = small[:, 48:64]
        gxb_half = small[:, 56:64]
        ls4 = small[:, 64:72]
        sums_a = small[:, 72:80].rearrange("p (t n) -> p t n", t=2)
        sums_b = small[:, 80:88].rearrange("p (t n) -> p t n", t=2)
        R = {name: dict(r=small[:, 88 + 6 * k:90 + 6 * k], half=small[:, 90 + 6 * k:92 + 6 * k],
                        square=small[:, 92 + 6 * k:94 + 6 * k], n=k + 1)
             for k, name in enumerate(("mem", "x", "u", "u2", "out"))}
        R["u"].update(hi=uT_hi, lo=uT_lo, v=V_LN1)
        R["u2"].update(hi=u2T_hi, lo=u2T_lo, v=V_LN2)
        lam = cols[:, V_LAM:V_LAM + 8]

        ps = ctx.enter_context(nc.psum_tensor("ps", [P, 8 * NW], F32))

        def bank(b, lo=0, hi=NW):
            return ps[:, b * NW + lo:b * NW + hi]

        raw_in = [sem(f"raw_in{k}") for k in range(SLOTS)]
        hi_ready = sem("hi_ready")
        lo_ready = sem("lo_ready")
        w_used = sem("w_used")
        acc_free = [sem("acc_free0"), sem("acc_free1")]
        z_tanh = sem("z_tanh")
        st_ready = sem("st_ready")
        tx_done = [sem("tx_done0"), sem("tx_done1")]
        tx_hi = [sem("tx_hi0"), sem("tx_hi1")]
        tx_free = [sem("tx_free0"), sem("tx_free1")]
        u_score, u_max, u_exp, u_pT, u_pTc, u_out, u_y, u_yT, u_hi, u_lo = (
            sem(n) for n in ("u_score", "u_max", "u_exp", "u_pT", "u_pTc", "u_out", "u_y", "u_yT", "u_hi", "u_lo"))
        r_score, r_dec, r_out, r_var, r_rstd, r_y, r_yT, r_hi, r_lo = (
            sem(n) for n in ("r_score", "r_dec", "r_out", "r_var", "r_rstd", "r_y", "r_yT", "r_hi", "r_lo"))
        l_sq, l_arg, l_conv, l_gate, l_own, l_tanh, l_nt, l_sqrt, l_y, l_hi, l_lo = (
            sem(n) for n in ("l_sq", "l_arg", "l_conv", "l_gate", "l_own", "l_tanh", "l_nt", "l_sqrt", "l_y", "l_hi", "l_lo"))
        sq_done, n_mean, n_root, r_made = sem("sq_done"), sem("n_mean"), sem("n_root"), sem("r_made")
        h_made, out_scaled, out_made = sem("h_made"), sem("out_scaled"), [sem("out_made0"), sem("out_made1")]
        dve_link = sem("dve_link")
        in_mem = [sem(f"in_mem{q}") for q in range(QUAD)]
        in_tables = sem("in_tables")
        in_x = [sem("in_x0"), sem("in_x1")]
        in_const, in_vec, in_res, in_g1, in_dec, in_gw, in_g2 = (
            sem(n) for n in ("in_const", "in_vec", "in_res", "in_g1", "in_dec", "in_gw", "in_g2"))
        spilled, in_h2, stored = sem("spilled"), sem("in_h2"), sem("stored")
        x_added = sem("x_added")
        pool_c, vec_ps, cols_ready, lam_abs, lam_e, lam_ready = (
            sem(n) for n in ("pool_c", "vec_ps", "cols_ready", "lam_abs", "lam_e", "lam_ready"))

        A0, B0 = 0, 4 * 1024
        QB, KB, VB, ZB = B0, B0 + 1536, B0 + 3072, B0 + 4608
        QM, ZM, GT = ZB + 512, ZB + 512 + 1024, ZB + 512 + 2048
        NG = D // NW
        NF = w_gate.shape[1] // NW

        def mem_unit(h):
            src = ([(qmT, 2 * h + c) for c in range(2)], [(mkT, 2 * h + c) for c in range(2)],
                   lambda kt: mv[:, kt, h * 256:(h + 1) * 256])
            return dict(scale=256 ** -0.5, blocks=[[(src, 0), (src, 1)]] * 2, mask=None, width=256,
                        s_at=(6 * NW, 6 * NW + 256), p_at=(7 * NW, 7 * NW + 256), o_at=6 * NW, y_at=7 * NW,
                        z=lambda t: zm[:, t, h * 256:(h + 1) * 256], kc=12 + 2 * h)

        def moba_unit(n):
            half, h = n // QUAD, n % QUAD
            src = ([(qaT[half], h)], [(kaT[half], h)], lambda kt: va[half][:, kt, h * HD:(h + 1) * HD])
            return dict(scale=HD ** -0.5, blocks=[[(src, 0)], [(src, 0), (src, 1)]], width=HD,
                        mask=(M_CAUSAL, M_NONE), s_at=(6 * NW, 6 * NW + P), p_at=(7 * NW, 7 * NW + P),
                        o_at=6 * NW, y_at=7 * NW, z=lambda t: za[half][:, t, h * HD:(h + 1) * HD], kc=n)

        def dil_unit(j):
            srcs = [([(qbT, g * QUAD + j)], [(kbT, g * QUAD + j)],
                     lambda kt, g=g: vb[:, g, kt, j * HD:(j + 1) * HD]) for g in range(3)]
            return dict(scale=HD ** -0.5, blocks=[[(s, 0) for s in srcs], [(s, kt) for s in srcs for kt in range(2)]],
                        width=HD, mask=("dil0", "dil1"), s_at=(4 * NW, 5 * NW), p_at=(4 * NW, 5 * NW),
                        o_at=7 * NW, y_at=4 * NW, z=lambda t: zb[:, t, j * HD:(j + 1) * HD], kc=8 + j, dil=True)

        def sb_at(unit, t):
            w0 = P * len(unit["blocks"][0])
            return (0, w0)[t], P * len(unit["blocks"][t])

        def masks(unit, t):
            m = unit["mask"][t]
            tiles = consts[:, C_MASK:C_END].rearrange("p (m c) -> p m c", c=P)
            if m == "dil0":
                return tiles[:, M_DIL + 1:M_DIL + 6:2, :]
            if m == "dil1":
                return tiles[:, M_DIL:M_DIL + 6, :]
            n = len(unit["blocks"][t])
            return tiles[:, m:m + n, :]

        def tiles_memkv():
            return [dict(w=w_mkv, col=NW * n, x="mem", post=("turn", mkT, n * QUAD) if n < 2 else ("take", mv[:, :, (n - 2) * NW:(n - 1) * NW]))
                    for n in range(4)]

        def tiles_attention():
            out_ = [dict(w=w_in, col=QM + NW * n, x="x", post=("turn", qmT, n * QUAD)) for n in range(2)]
            out_ += [dict(w=w_in, col=ZM + NW * n, x="x", post=("silu", zm[:, :, n * NW:(n + 1) * NW])) for n in range(2)]
            for half in range(2):
                c = A0 + half * NW
                four = [dict(w=w_in, col=c, x="x", post=("rope", qaT[half], 0)),
                        dict(w=w_in, col=c + 1024, x="x", post=("rope", kaT[half], 0)),
                        dict(w=w_in, col=c + 2048, x="x", post=("take", va[half][:, :, :])),
                        dict(w=w_in, col=c + 3072, x="x", post=("silu", za[half][:, :, :]))]
                for n in range(4):
                    four[n]["unit"] = mem_unit(n) if half == 0 else moba_unit(n)
                out_ += four
            ten = [dict(w=w_in, col=QB + NW * g, x="x", post=("rope", qbT, g * QUAD)) for g in range(3)]
            ten += [dict(w=w_in, col=KB + NW * g, x="x", post=("rope", kbT, g * QUAD)) for g in range(3)]
            ten += [dict(w=w_in, col=VB + NW * g, x="x", post=("take", vb[:, g])) for g in range(3)]
            ten += [dict(w=w_in, col=ZB, x="x", post=("silu", zb[:, :, :]))]
            for n in range(4):
                ten[n]["unit"] = moba_unit(QUAD + n)
            return out_ + ten

        def tiles_merge(n, first=False):
            out_ = [dict(w=w_in, col=n * NW + (GT + b * D), x="x", post=("gate", b)) for b in (2, 0, 1)]
            out_ += [dict(w=w_pm, col=n * NW, x="y", k0=12, hcs=4, post=("mix", 2, "first")),
                     dict(w=w_pa, col=n * NW, x="y", k0=0, hcs=4, post=("mix", 0, "more")),
                     dict(w=w_pb, col=n * NW, x="y", k0=8, hcs=4, per=1, post=("mix", 1, "last", n))]
            if first:
                for k in range(4):
                    out_[k]["unit"] = dil_unit(k)
            return out_

        def tiles_two():
            out_ = []
            for half in range(2):
                out_ += [dict(w=w_in2, col=half * NW, x="u", post=("turn", lxT, half * QUAD)),
                         dict(w=w_in2, col=1024 + half * NW, x="u", post=("turn", lgT, half * QUAD))]
            for half in range(2):
                c = 2048 + half * NW
                out_ += [dict(w=w_in2, col=c, x="u", post=("rope", qrT[half], 0)),
                         dict(w=w_in2, col=c + 1024, x="u", post=("rope", krT[half], 0)),
                         dict(w=w_in2, col=c + 2048, x="u", post=("take", vr[half][:, :, :])),
                         dict(w=w_in2, col=c + 3072, x="u", post=("silu", gr[half][:, :, :]))]
            for n in range(8):
                out_[4 + n]["lru"] = n
            for n in range(4):
                out_[8 + n]["ret"] = n
            return out_

        def tiles_ffn(n):
            return [dict(w=w_gate, col=n * NW, x="u2", post=("ffg",)),
                    dict(w=w_up, col=n * NW, x="u2", post=("ffu", n))]

        def merge_last(n):
            return dict(post=("mix", 1, "last", n), par=1)

        def ffn_last(n):
            return dict(post=("ffu", n), par=1)

        HCS = 8
        PARTS = {"mem": (memT_hi, memT_lo), "x": (xT_hi, xT_lo), "y": (yT_hi, yT_lo), "m": (mrgT_hi, mrgT_lo),
                 "u": (uT_hi, uT_lo), "y2": (y2T_hi, y2T_lo), "u2": (u2T_hi, u2T_lo), "ff": (ffT_hi, ffT_lo)}

        def pos(tile, p):
            return min(p, len(chunks(tile)) - 1)

        def res_tiles(weight, x, dst, k=0, hcs=HCS, what=""):
            return [dict(w=weight, col=(k * 2 + m) * NW, x=x, hcs=hcs, post=("res", dst, k * 2 + m, what)) for m in range(2)]

        def tiles_out2():
            one, two = res_tiles(w_out2, "y2", h2, 0, what="u2")
            three, four = res_tiles(w_out2, "y2", h2, 1, what="u2")
            cut = lambda tile, par, a, b, follow: dict(tile, par=par, part=(a, b), follow=follow)
            return [cut(one, 0, 0, 6, True), cut(two, 1, 0, 6, False), cut(one, 0, 6, 7, False), cut(two, 1, 6, 7, False),
                    cut(one, 0, 7, 8, False), cut(two, 1, 7, 8, True), three, four]

        def ret_y_bank(n):
            return 5 if n >= QUAD else 6

        def chunks(tile):
            return range(*tile.get("part", (0, tile.get("hcs", HCS))))

        def tail_hooks(tiles, key, at_chunk):
            n = 0
            for tile in tiles:
                m = len(chunks(tile))
                tile[key] = {k - n: f for k, f in at_chunk.items() if n <= k < n + m}
                n += m

        G_X = 8 * 26 + 36 * (NG - 1) + 24
        G_MERGE = 8 * 26 + 36 * NG
        G_U = 8 * 26 + 36 * NG + 8 * NG + 8 * 12
        G_U2 = G_U + 8 * NG + 16 * NF

        block = ctx.enter_context(nc.Block())

        @block.sync
        def _(sp):
            w = Walk()

            def load(tile, then={}):
                per = tile.get("per", 2)
                src = tile["w"].rearrange("(c p) n -> p c n", p=P)
                if w.loop:
                    sp.to_reg(tile["col"] * 4)
                for h in chunks(tile):
                    s = w.n["g"] % SLOTS
                    sp.wait_ge(lo_ready, w("g", 1))
                    sp.dma_start(raw[:, s, 0:per], src[:, h * per:(h + 1) * per, bass.ds(tile["col"], NW)])\
                      .then_inc(raw_in[s], 16)
                    w.step("g")
                    if h in then:
                        then[h]()

            def load_all(tiles):
                for tile in tiles:
                    load(tile)

            def load_mem(q):
                c = slice(q * NW, (q + 1) * NW)
                sp.dma_start(mem_tok[:, :, c], mem.rearrange("(t p) n -> p t n", p=P)[:, :, c]).then_inc(in_mem[q], 16)

            sp.dma_start(ident, consts_d[:, C_ID:C_ID + P]).then_inc(in_const, 16)
            sp.dma_start(vec_a[:, :], vecs[0:P]).then_inc(in_vec, 16)
            sp.dma_start(vec_b[0:V_END - P, :], vecs[P:V_END]).then_inc(in_vec, 16)
            load_mem(0)
            first, *rest = tiles_memkv()
            load(first, {0: lambda: load_mem(1), 1: lambda: load_mem(2), 2: lambda: load_mem(3)})
            sp.dma_start(consts[:, C_ID + P:], consts_d[:, C_ID + P:]).then_inc(in_tables, 16)
            for t in range(NT):
                sp.dma_start(x_tok[:, t], x[t * P:(t + 1) * P, :]).then_inc(in_x[t], 16)
            load_all(rest + tiles_attention() + tiles_merge(0))
            w.rounds(sp, NG - 1, lambda i: load_all(tiles_merge(i + 1)))
            w.rounds(sp, NG // 2, lambda i: load_all(res_tiles(w_out, "m", None, i)))
            load_all(tiles_two())
            load_all(tiles_out2())
            w.rounds(sp, NF, lambda i: load_all(tiles_ffn(i)))
            w.rounds(sp, NG // 2, lambda i: load_all(res_tiles(w_down, "ff", None, i, FC // 2)))
            for t in range(NT):
                for m in range(2):
                    sp.wait_ge(out_made[t], m + 1)
                    c = slice(m * D // 2, (m + 1) * D // 2)
                    sp.dma_start(out[t * P:(t + 1) * P, c], h2[:, t, c]).then_inc(stored, 16)
            sp.wait_ge(stored, 32 * NT)

        @block.gpsimd
        def _(pool):
            nc.gpsimd.memset(mneg_c[:, :], -0.5).then_inc(pool_c, 1)
            pool.wait_ge(pool_c, 1)

            def norm_root(k, dst):
                pool.wait_ge(n_mean, k + 1)
                nc.gpsimd.tensor_tensor(dst, meansq, mneg_c[:, :], ALU.pow).then_inc(n_root, 1)

            def spread(dst, g, s):
                pool.dma_start(dst, g.rearrange("(a n) -> a n", a=1).broadcast_to([P, D])).then_inc(s, 16)

            def ret_root(n):
                pool.wait_ge(r_var, n + 1)
                nc.gpsimd.tensor_tensor(ret_rstd, ret_var, mneg_c[:, :], ALU.pow).then_inc(r_rstd, 1)

            norm_root(0, R["mem"]["r"])
            norm_root(1, R["x"]["r"])
            pool.wait_ge(w_used, G_X + SLOTS)
            for t in range(NT):
                pool.dma_start(x1[:, t], x[t * P:(t + 1) * P, :]).then_inc(in_res, 16)
            spread(g_row1[:, :], fin1_g, in_g1)
            pool.wait_ge(w_used, G_MERGE + SLOTS)
            pool.dma_start(decay[:, :, :], decay_d).then_inc(in_dec, 16)
            pool.dma_start(ga_w[:, :, :], gate_a.rearrange("n c d -> c n d")).then_inc(in_gw, 16)
            pool.dma_start(gx_w[:, :, :], gate_x.rearrange("n c d -> c n d")).then_inc(in_gw, 16)
            norm_root(2, r_first)
            norm_root(3, R["u"]["r"])
            pool.wait_ge(h_made, 1)
            for t in range(NT):
                pool.dma_start(spill[t * P:(t + 1) * P, :], x1[:, t]).then_inc(spilled, 16)
            for n in range(QUAD):
                ret_root(n)
            pool.wait_ge(spilled, 16 * NT)
            pool.wait_ge(w_used, G_U + SLOTS)
            for t in range(NT):
                pool.dma_start(h2[:, t], spill[t * P:(t + 1) * P, :]).then_inc(in_h2, 16)
            for n in range(QUAD, 2 * QUAD):
                ret_root(n)
            norm_root(4, R["u2"]["r"])
            pool.wait_ge(w_used, G_U2 + SLOTS)
            spread(g_row2[:, :], fin2_g, in_g2)
            norm_root(5, R["out"]["r"])

        @block.scalar
        def _(act):
            w = Walk()

            def split(tile):
                s, per = w.n["g"] % SLOTS, tile.get("per", 2)
                act.wait_ge(raw_in[s], w.slot_uses())
                act.wait_ge(w_used, w("g", 1))
                nc.scalar.activation(w_hi[:, s, 0:per], raw[:, s, 0:per], ACT.Copy).then_inc(hi_ready, 1)
                w.step("g")

            def squares(src, sums, ready):
                for t in range(NT):
                    ready(t)
                    if w.n["sq"]:
                        act.wait_ge(sq_done, w.n["sq"])
                    nc.scalar.activation(sq_out[:, 0:D], src[:, t], ACT.Square, accum_out=sums[:, t:t + 1]).then_inc(sq_done, 1)
                    w.step("sq")

            def tile_squares(prev):
                _, dst, n, what = prev["post"]
                act.wait_ge(sq_done, w.n["sq"])
                for t in range(NT):
                    ins = nc.scalar.activation(sq_out[:, t * NW:(t + 1) * NW], dst[:, t, n * NW:(n + 1) * NW], ACT.Square,
                                               accum_out=sums_a[:, t, n:n + 1])
                    if what == "u":
                        ins = nc.scalar.activation(sq_out[:, (NT + t) * NW:(NT + t + 1) * NW], stage[:, t], ACT.Square,
                                                   accum_out=sums_b[:, t, n:n + 1])
                ins.then_inc(sq_done, 1)
                w.step("sq")

            def job_hi(q, hi, factors):
                pair = q % 2
                act.wait_ge(tx_done[pair], w(f"j{pair}", 1))
                for c in range(QUAD):
                    kc = q * QUAD + c
                    ins = nc.scalar.activation(hi[:, kc], bank(4 + 2 * pair, c * S, (c + 1) * S), ACT.Copy,
                                               scale=factors[:, kc:kc + 1])
                ins.then_inc(tx_hi[pair], 1)
                w.step(f"j{pair}", f"h{pair}")

            def unit_exp(unit):
                act.wait_ge(u_max, w("u", 1))
                for t in range(NT):
                    a, n = sb_at(unit, t)
                    src = scores[:, a:a + n] if unit["mask"] else ps[:, unit["s_at"][t]:unit["s_at"][t] + n]
                    ins = nc.scalar.activation(scores[:, a:a + n], src, ACT.Exp, bias=negmax[:, t:t + 1],
                                               scale=unit["scale"], accum_out=rowsum[:, t:t + 1])
                ins.then_inc(u_exp, 1)

            def unit_copy(unit):
                act.wait_ge(u_pT, w("u", 1))
                for t in range(NT):
                    a, n = sb_at(unit, t)
                    ins = nc.scalar.activation(probsT[:, a:a + n], ps[:, unit["p_at"][t]:unit["p_at"][t] + n], ACT.Copy)
                ins.then_inc(u_pTc, 1)

            def unit_hi(unit):
                act.wait_ge(u_yT, w("u", 1))
                kc, n = unit["kc"], unit["width"] // P
                nc.scalar.activation(yT_hi[:, kc:kc + n], ps[:, unit["y_at"]:unit["y_at"] + n * S].rearrange("p (c s) -> p c s", s=S),
                                     ACT.Copy, scale=0.5).then_inc(u_hi, 1)
                w.step("u")

            def ret_hi(n):
                act.wait_ge(r_yT, n + 1)
                nc.scalar.activation(y2T_hi[:, 8 + n], bank(ret_y_bank(n), 0, S), ACT.Copy, scale=gn_half[:, n:n + 1]).then_inc(r_hi, 1)

            def lru_square(n):
                if n:
                    act.wait_ge(l_y, n)
                nc.scalar.activation(gelu, lgT[:, n], ACT.Square).then_inc(l_sq, 1)

            def lru_tanh(n):
                if n == 0:
                    act.wait_ge(lam_ready, 1)
                act.wait_ge(l_arg, n + 1)
                nc.scalar.activation(gelu, gelu, ACT.Tanh, scale=float(np.sqrt(2 / np.pi)))
                act.wait_ge(l_gate, n + 1)
                nc.scalar.activation(lru_t, bank(7, 0, S), ACT.Tanh, scale=0.5, bias=gab_half[:, n:n + 1]).then_inc(l_own, 1)
                nc.scalar.activation(lru_i, bank(7, S, 2 * S), ACT.Tanh, scale=0.5, bias=gxb_half[:, n:n + 1])
                act.wait_ge(l_own, n + 1)
                nc.scalar.activation(lru_t, lru_t, ACT.Tanh, scale=ls4[:, n:n + 1], bias=ls4[:, n:n + 1]).then_inc(l_tanh, 1)

            def lru_sqrt(n):
                act.wait_ge(l_nt, n + 1)
                nc.scalar.activation(lru_root, lru_root, ACT.Sqrt).then_inc(l_sqrt, 1)

            def lru_hi(n):
                act.wait_ge(l_y, n + 1)
                nc.scalar.activation(y2T_hi[:, n], lru_y, ACT.Copy, scale=0.5).then_inc(l_hi, 1)

            def post(prev, done):
                if prev is None:
                    return
                kind, par = prev["post"], prev["par"]
                if kind[0] in ("take", "silu", "gate", "ffg"):
                    act.wait_ge(w_used, w("g", SLOTS - done))
                    act.wait_ge(r_made, R[prev["x"]]["n"])
                    dst = gates[:, kind[1]] if kind[0] == "gate" else ff_g if kind[0] == "ffg" else kind[1]
                    for t in range(NT):
                        if kind[0] == "take":
                            ins = nc.scalar.activation(dst[:, t], bank(2 * par + t), ACT.Copy, scale=R[prev["x"]]["r"][:, t:t + 1])
                        else:
                            ins = nc.scalar.activation(dst[:, t], bank(2 * par + t), ACT.Tanh, scale=R[prev["x"]]["half"][:, t:t + 1])
                    ins.then_inc(acc_free[par] if kind[0] in ("take", "gate") else z_tanh, 1)
                w.count_post(prev)

            def post_job(prev):
                if prev is None:
                    return
                kind = prev["post"]
                if kind[0] == "res":
                    if through_stage(kind):
                        act.wait_ge(st_ready, w("st", 1))
                    else:
                        act.wait_ge(acc_free[prev["par"]], w(f"a{prev['par']}"))
                    tile_squares(prev)
                if kind[0] == "res" and through_stage(kind):
                    hi, v = R[kind[3]]["hi"], R[kind[3]]["v"]
                    act.wait_ge(tx_done[0], w("j0", 1))
                    for c in range(QUAD):
                        kc = kind[2] * QUAD + c
                        ins = nc.scalar.activation(hi[:, kc], bank(4, c * S, (c + 1) * S), ACT.Copy, scale=cols[:, v + kc:v + kc + 1])
                    ins.then_inc(tx_hi[0], 1)
                elif through_stage(kind):
                    act.wait_ge(tx_done[0], w("j0", 1))
                    src = ps[:, 4 * NW:6 * NW].rearrange("p (c s) -> p c s", s=S)
                    if split_job(kind):
                        dst = ffT_hi if kind[0] == "ffu" else mrgT_hi
                        nc.scalar.activation(dst[:, bass.ds(kind[-1] * QUAD, QUAD)], src, ACT.Copy, scale=0.5).then_inc(tx_hi[0], 1)
                    else:
                        nc.scalar.activation(kind[1][:, kind[2]:kind[2] + QUAD], src, ACT.Copy).then_inc(tx_free[0], 1)
                w.count_job(prev)

            def run(tile, prev, hooks=()):
                unit = tile.get("unit")
                for h, _ in enumerate(chunks(tile)):
                    split(tile)
                    if "lru" in tile and h == 1:
                        lru_square(tile["lru"])
                    if h == pos(tile, 3):
                        post(prev, h + 1)
                    if unit and h == pos(tile, 4):
                        unit_exp(unit)
                    if unit and h == pos(tile, 5):
                        unit_copy(unit)
                    if "lru" in tile and h == 5:
                        lru_tanh(tile["lru"])
                    if "lru" in tile and h == 6:
                        lru_sqrt(tile["lru"])
                    if h == pos(tile, 7 if unit else 6):
                        post_job(prev)
                    for f in dict(hooks).get(h, ()):
                        f()
                if unit:
                    unit_hi(unit)
                if "ret" in tile:
                    ret_hi(tile["ret"])
                if "lru" in tile:
                    lru_hi(tile["lru"])
                return tile

            def chain(tiles, prev):
                for n, tile in enumerate(tiles):
                    tile.setdefault("par", n % 2)
                    prev = run(tile, prev if tile.get("follow", True) else None, tile.get("act_hooks", ()))
                return prev

            def jobs(hi, v, *quads):
                return [lambda q=q: job_hi(q, hi, cols[:, v:v + KC]) for q in quads]

            def mem_in():
                for q in range(QUAD):
                    act.wait_ge(in_mem[q], 16)

            def log_sigmoid_exp():
                nc.scalar.activation(lamb[:, 0], lam, ACT.Abs).then_inc(lam_abs, 1)
                act.wait_ge(lam_abs, 1)
                nc.scalar.activation(lamb[:, 1], lamb[:, 0], ACT.Exp, scale=-1.0).then_inc(lam_e, 1)

            four = tiles_memkv()
            four[0]["act_hooks"] = {0: jobs(memT_hi, V_MEM, 1), 2: jobs(memT_hi, V_MEM, 2), 3: jobs(memT_hi, V_MEM, 3),
                                    5: [mem_in, lambda: squares(mem_tok, sumsq_m, lambda t: None)]}
            four[1]["act_hooks"] = {7: [lambda: squares(x_tok, sumsq_x, lambda t: act.wait_ge(in_x[t], 16))]}
            for n in (2, 3):
                four[n]["act_hooks"] = {6: jobs(xT_hi, V_IN, 2 * n - 4), 7: jobs(xT_hi, V_IN, 2 * n - 3)}
            last = four[3]["act_hooks"].pop(7)
            four[3]["act_hooks"][5] = [log_sigmoid_exp]
            act.wait_ge(cols_ready, 1)
            job_hi(0, memT_hi, cols[:, V_MEM:V_MEM + KC])
            prev = chain(four, None)
            tiles = tiles_attention()
            tiles[0]["act_hooks"] = {1: last}
            prev = chain(tiles, prev)
            prev = chain(tiles_merge(0, first=True), prev)
            w.rounds(act, NG - 1, lambda i: chain(tiles_merge(i + 1), merge_last(i)))
            prev = merge_last(NG - 1)
            for k in range(NG // 2):
                prev = chain(res_tiles(w_out, "m", x1, k, what="u"), prev)
            tiles = tiles_two()
            tiles[4]["act_hooks"] = {7: [lambda: act.wait_ge(spilled, 16 * NT)]}
            prev = chain(tiles, prev)
            tiles = tiles_out2()
            tiles[0]["act_hooks"] = {}
            tail_hooks(tiles, "act_hooks", {7: [lambda: ret_hi(4)], 10: [lambda: ret_hi(5)], 13: [lambda: ret_hi(6)], 14: [lambda: ret_hi(7)]})
            prev = chain(tiles, prev)
            chain(tiles_ffn(0), prev)
            w.rounds(act, NF - 1, lambda i: chain(tiles_ffn(i + 1), ffn_last(i)))
            prev = ffn_last(NF - 1)
            for k in range(NG // 2):
                prev = chain(res_tiles(w_down, "ff", h2, k, FC // 2, "out"), prev)
            act.wait_ge(x_added, 1)
            tile_squares(prev)
            act.wait_ge(out_scaled, NG)
            act.wait_ge(n_root, 6)
            for m in range(2):
                c = slice(m * D // 2, (m + 1) * D // 2)
                nc.scalar.activation(h2[:, 1, c], h2[:, 1, c], ACT.Copy, scale=R["out"]["r"][:, 1:2]).then_inc(out_made[1], 1)

        @block.vector
        def _(dve):
            w = Walk()
            dve.sem_inc(lo_ready, SLOTS)

            def link(ins):
                ins.then_inc(dve_link, 1)
                w.step("link")
                dve.wait_ge(dve_link, w("link"))

            def split(tile):
                s, per = w.n["g"] % SLOTS, tile.get("per", 2)
                dve.wait_ge(hi_ready, w("g", 1))
                nc.vector.tensor_tensor(w_lo[:, s, 0:per], raw[:, s, 0:per], w_hi[:, s, 0:per].bitcast(F32), ALU.subtract)\
                  .then_inc(lo_ready, 1)
                w.step("g")

            def root(sums, k, per=None):
                if per is None:
                    ins = nc.vector.tensor_scalar(meansq, sums, 1.0 / D, EPS, ALU.mult, ALU.add)
                else:
                    link(nc.vector.tensor_tensor(meansq, sums, per, ALU.mult))
                    link(nc.vector.tensor_tensor(meansq, meansq, per, ALU.mult))
                    ins = nc.vector.tensor_scalar(meansq, meansq, 1.0 / D, EPS, ALU.mult, ALU.add)
                ins.then_inc(n_mean, 1)
                dve.wait_ge(n_root, k + 1)

            def factors(name):
                f = R[name]
                ins = nc.vector.tensor_tensor(f["square"], f["r"], f["r"], ALU.mult)
                if name in ("x", "u"):
                    for t in range(NT):
                        nc.vector.tensor_scalar(rot[:, t, 0:64], consts[:, C_COS + t * 64:C_COS + (t + 1) * 64],
                                                f["r"][:, t:t + 1], None, ALU.mult)
                        ins = nc.vector.tensor_scalar(rot[:, t, 64:192], consts[:, C_SIN + t * 128:C_SIN + (t + 1) * 128],
                                                      f["r"][:, t:t + 1], None, ALU.mult)
                link(ins)
                nc.vector.tensor_scalar(f["half"], f["r"], 0.5, None, ALU.mult).then_inc(r_made, 1)

            def sum_up(sums):
                link(nc.vector.reduce_sum(sum_ab, sums, AX))

            def job_lo(q, hi, lo, factors):
                pair = q % 2
                dve.wait_ge(tx_hi[pair], w(f"h{pair}", 1))
                for c in range(QUAD):
                    kc = q * QUAD + c
                    ins = nc.vector.scalar_tensor_tensor(lo[:, kc], bank(4 + 2 * pair, c * S, (c + 1) * S), factors[:, kc:kc + 1],
                                                         hi[:, kc].bitcast(F32), ALU.mult, ALU.subtract)
                ins.then_inc(tx_free[pair], 1)
                w.step(f"j{pair}", f"h{pair}")

            def unit_mask(unit):
                dve.wait_ge(u_score, w("u", 1))
                for t in range(NT):
                    a, n = sb_at(unit, t)
                    src = ps[:, unit["s_at"][t]:unit["s_at"][t] + n]
                    if unit["mask"]:
                        link(nc.vector.tensor_tensor(scores[:, a:a + n].rearrange("p (m c) -> p m c", c=P),
                                                     src.rearrange("p (m c) -> p m c", c=P), masks(unit, t), ALU.add))
                        src = scores[:, a:a + n]
                    last = nc.vector.reduce_max(rowmax[:, t:t + 1], src, AX)
                link(last)
                nc.vector.tensor_scalar(negmax, rowmax, -unit["scale"], None, ALU.mult).then_inc(u_max, 1)

            def unit_norm(unit):
                dve.wait_ge(u_exp, w("u", 1))
                link(nc.vector.reciprocal(rinv, rowsum))
                link(nc.vector.tensor_tensor(rinv, rinv, R["x"]["r"], ALU.mult))
                dve.wait_ge(u_out, w("u", 1))
                n = unit["width"]
                for t in range(NT):
                    ins = nc.vector.scalar_tensor_tensor(
                        y_tok[:, t, 0:n], ps[:, unit["o_at"] + t * n:unit["o_at"] + (t + 1) * n], rinv[:, t:t + 1],
                        unit["z"](t), ALU.mult, ALU.mult)
                ins.then_inc(u_y, 1)

            def unit_lo(unit):
                dve.wait_ge(u_hi, w("u", 1))
                kc, n = unit["kc"], unit["width"] // P
                nc.vector.scalar_tensor_tensor(
                    yT_lo[:, kc:kc + n], ps[:, unit["y_at"]:unit["y_at"] + n * S].rearrange("p (c s) -> p c s", s=S), 0.5,
                    yT_hi[:, kc:kc + n].bitcast(F32), ALU.mult, ALU.subtract).then_inc(u_lo, 1)
                w.step("u")

            def ret_decay(n):
                dve.wait_ge(r_score, n + 1)
                if n == 0:
                    dve.wait_ge(in_dec, 16)
                nc.vector.tensor_tensor(probsT[:, 0:S], bank(6, 0, S), decay[:, n], ALU.mult)
                nc.vector.tensor_tensor(probsT[:, S:S + P], bank(6, S, S + P), decay[:, n, 0:P], ALU.mult).then_inc(r_dec, 1)

            def ret_norm(n):
                dve.wait_ge(r_out, n + 1)
                for t in range(NT):
                    ins = nc.vector.bn_stats(stats[:, t], bank(7, t * HD, (t + 1) * HD))
                link(ins)
                for t in range(NT):
                    ins = nc.vector.bn_aggr(moments[:, t], stats[:, t])
                link(ins)
                nc.vector.tensor_scalar(ret_var, moments[:, :, 1], EPS, None, ALU.add).then_inc(r_var, 1)
                dve.wait_ge(r_rstd, n + 1)
                link(nc.vector.tensor_tensor(ret_var, ret_rstd, R["u"]["r"], ALU.mult))
                for t in range(NT):
                    ins = nc.vector.tensor_scalar(y_tok[:, t, 0:HD], bank(7, t * HD, (t + 1) * HD), moments[:, t, 0:1],
                                                  ret_var[:, t:t + 1], ALU.subtract, ALU.mult)
                link(ins)
                half, h = n // QUAD, n % QUAD
                nc.vector.tensor_tensor(y_tok[:, :, 0:HD], y_tok[:, :, 0:HD], gr[half][:, :, h * HD:(h + 1) * HD], ALU.mult)\
                  .then_inc(r_y, 1)

            def ret_lo(n):
                dve.wait_ge(r_hi, n + 1)
                nc.vector.scalar_tensor_tensor(y2T_lo[:, 8 + n], bank(ret_y_bank(n), 0, S), gn_half[:, n:n + 1],
                                               y2T_hi[:, 8 + n].bitcast(F32), ALU.mult, ALU.subtract).then_inc(r_lo, 1)

            def lru_conv(n):
                xin = lxT[:, n]
                tap = lambda k: cols[:, V_CONVW + 8 * k + n:V_CONVW + 8 * k + n + 1]
                dve.wait_ge(l_sq, n + 1)
                link(nc.vector.tensor_scalar(gelu, gelu, 0.044715, 1.0, ALU.mult, ALU.add))
                nc.vector.tensor_tensor(gelu, gelu, lgT[:, n], ALU.mult).then_inc(l_arg, 1)
                link(nc.vector.tensor_scalar(lru_u, xin, tap(3), cols[:, V_CONVB + n:V_CONVB + n + 1], ALU.mult, ALU.add))
                for d in (1, 2, 3):
                    ins = nc.vector.scalar_tensor_tensor(lru_u[:, d:S], xin[:, 0:S - d], tap(3 - d), lru_u[:, d:S], ALU.mult, ALU.add)
                    if d < 3:
                        link(ins)
                ins.then_inc(l_conv, 1)

            def lru_decay(n):
                dve.wait_ge(l_tanh, n + 1)
                nc.vector.tensor_scalar(lru_root, lru_t, -1.0, 1e-30, ALU.mult, ALU.max).then_inc(l_nt, 1)
                link(nc.vector.tensor_scalar(lru_r, lru_t, -1.0, 1.0, ALU.mult, ALU.add))
                link(nc.vector.reciprocal(lru_r, lru_r))
                nc.vector.scalar_tensor_tensor(lru_a, lru_t, 1.0, lru_r, ALU.add, ALU.mult)
                link(nc.vector.scalar_tensor_tensor(lru_i, lru_i, 1.0, lru_u, ALU.add, ALU.mult))
                link(nc.vector.tensor_tensor(lru_i, lru_i, lru_r, ALU.mult))
                link(nc.vector.scalar_tensor_tensor(lru_y, gelu, 1.0, lgT[:, n], ALU.add, ALU.mult))

            def lru_scan(n):
                dve.wait_ge(l_sqrt, n + 1)
                link(nc.vector.tensor_tensor(lru_i, lru_i, lru_root, ALU.mult))
                link(nc.vector.tensor_tensor_scan(lru_r, lru_a, lru_i, 0.0, ALU.mult, ALU.add))
                nc.vector.tensor_tensor(lru_y, lru_y, lru_r, ALU.mult).then_inc(l_y, 1)

            def lru_lo(n):
                dve.wait_ge(l_hi, n + 1)
                nc.vector.scalar_tensor_tensor(y2T_lo[:, n], lru_y, 0.5, y2T_hi[:, n].bitcast(F32),
                                               ALU.mult, ALU.subtract).then_inc(l_lo, 1)

            def rotate(par):
                for t in range(NT):
                    cos = rot[:, t, 0:64]
                    sin = rot[:, t, 64:192].rearrange("p (a d) -> p a d", a=2)
                    acc = bank(2 * par + t)
                    nc.vector.tensor_tensor(stage[:, t].rearrange("p (a d) -> p a d", d=64), acc.rearrange("p (a d) -> p a d", d=64),
                                            cos[:, None, :].broadcast_to([P, 2 * QUAD, 64]), ALU.mult)
                    a4 = acc.rearrange("p (h a d) -> p h a d", a=2, d=64)
                    t4 = tmp[:, t].rearrange("p (h a d) -> p h a d", a=2, d=64)
                    for a in range(2):
                        last = nc.vector.tensor_tensor(t4[:, :, a], a4[:, :, 1 - a],
                                                       sin[:, a][:, None, :].broadcast_to([P, QUAD, 64]), ALU.mult)
                link(last)
                nc.vector.tensor_tensor(stage[:, :, :], stage[:, :, :], tmp[:, :, :], ALU.add).then_inc(st_ready, 1)

            def post(prev, done, signal=None):
                if prev is None:
                    return
                kind, par = prev["post"], prev["par"]
                accs = [bank(2 * par + t) for t in range(NT)]
                if kind[0] in ("silu", "ffg"):
                    dst = kind[1] if kind[0] == "silu" else ff_g
                    dve.wait_ge(z_tanh, w("z", 1))
                    for t in range(NT):
                        last = nc.vector.scalar_tensor_tensor(dst[:, t], dst[:, t], 1.0, accs[t], ALU.add, ALU.mult)
                    last.then_inc(acc_free[par], 1)
                elif kind[0] not in ("take", "gate"):
                    dve.wait_ge(w_used, w("g", SLOTS - done))
                if through_stage(kind) or kind[0] == "mix" and kind[2] == "first":
                    if w.n["j0"]:
                        dve.wait_ge(tx_done[0], w("j0"))
                if kind[0] == "turn":
                    for t in range(NT):
                        last = nc.vector.tensor_scalar(stage[:, t], accs[t], R[prev["x"]]["r"][:, t:t + 1], None, ALU.mult)
                    last.then_inc(st_ready, 1)
                if kind[0] == "rope":
                    rotate(par)
                if kind[0] == "mix":
                    gate = gates[:, kind[1]]
                    to = stage if kind[2] == "first" else tmp
                    for t in range(NT):
                        last = nc.vector.scalar_tensor_tensor(to[:, t], gate[:, t], 1.0, accs[t], ALU.add, ALU.mult)
                    if kind[2] == "last":
                        link(last)
                        nc.vector.tensor_tensor(stage[:, :, :], stage[:, :, :], tmp[:, :, :], ALU.add).then_inc(st_ready, 1)
                    else:
                        last.then_inc(acc_free[par], 1)
                        dve.wait_ge(acc_free[par], w(f"a{par}", 1))
                        if kind[2] == "more":
                            link(nc.vector.tensor_tensor(stage[:, :, :], stage[:, :, :], tmp[:, :, :], ALU.add))
                if kind[0] == "ffu":
                    for t in range(NT):
                        last = nc.vector.scalar_tensor_tensor(stage[:, t], ff_g[:, t], R["u2"]["square"][:, t:t + 1], accs[t],
                                                              ALU.mult, ALU.mult)
                    last.then_inc(st_ready, 1)
                if kind[0] == "res":
                    _, dst, n, what = kind
                    cs = slice(n * NW, (n + 1) * NW)
                    for t in range(NT):
                        last = nc.vector.tensor_tensor(dst[:, t, cs], dst[:, t, cs], accs[t], ALU.add)
                    if what == "u":
                        link(last)
                        dve.wait_ge(sq_done, w.n["sq"])
                        for t in range(NT):
                            last = nc.vector.tensor_tensor(stage[:, t], dst[:, t, cs], g_row1[:, cs], ALU.mult)
                    last.then_inc(st_ready if what != "out" else signal or acc_free[par], 1)
                if signal is None:
                    w.count_post(prev)

            def post_job(prev):
                if prev is None:
                    return
                kind = prev["post"]
                if kind[0] == "res":
                    w.step("sq")
                    if kind[3] == "out":
                        scale_out(kind[2])
                if kind[0] == "res" and through_stage(kind):
                    f = R[kind[3]]
                    dve.wait_ge(tx_hi[0], w("h0", 1))
                    for c in range(QUAD):
                        kc = kind[2] * QUAD + c
                        ins = nc.vector.scalar_tensor_tensor(
                            f["lo"][:, kc], bank(4, c * S, (c + 1) * S), cols[:, f["v"] + kc:f["v"] + kc + 1],
                            f["hi"][:, kc].bitcast(F32), ALU.mult, ALU.subtract)
                    ins.then_inc(tx_free[0], 1)
                elif through_stage(kind) and split_job(kind):
                    hi, lo = (ffT_hi, ffT_lo) if kind[0] == "ffu" else (mrgT_hi, mrgT_lo)
                    c = bass.ds(kind[-1] * QUAD, QUAD)
                    dve.wait_ge(tx_hi[0], w("h0", 1))
                    nc.vector.scalar_tensor_tensor(lo[:, c], ps[:, 4 * NW:6 * NW].rearrange("p (c s) -> p c s", s=S), 0.5,
                                                   hi[:, c].bitcast(F32), ALU.mult, ALU.subtract).then_inc(tx_free[0], 1)
                w.count_job(prev)

            def run(tile, prev, hooks=()):
                unit = tile.get("unit")
                for h, _ in enumerate(chunks(tile)):
                    split(tile)
                    if "lru" in tile and h == 2:
                        lru_conv(tile["lru"])
                    if unit and h == pos(tile, 4):
                        unit_mask(unit)
                    if h == pos(tile, 5 if unit else 3):
                        post(prev, h + 1)
                    if "ret" in tile and h == 4:
                        ret_decay(tile["ret"])
                    if "lru" in tile and h == 6:
                        lru_decay(tile["lru"])
                    if h == pos(tile, 7 if unit else 6):
                        post_job(prev)
                    for f in dict(hooks).get(h, ()):
                        f()
                if unit:
                    unit_norm(unit)
                    unit_lo(unit)
                if "ret" in tile:
                    ret_norm(tile["ret"])
                if "lru" in tile:
                    lru_scan(tile["lru"])
                if "ret" in tile:
                    ret_lo(tile["ret"])
                if "lru" in tile:
                    lru_lo(tile["lru"])
                return tile

            def chain(tiles, prev):
                for n, tile in enumerate(tiles):
                    tile.setdefault("par", n % 2)
                    prev = run(tile, prev if tile.get("follow", True) else None, tile.get("dve_hooks", ()))
                return prev

            def log_sigmoid():
                dve.wait_ge(lam_e, 1)
                e, den, s_, s2, acc = (lamb[:, k] for k in (1, 2, 3, 4, 5))
                link(nc.vector.tensor_scalar(den, e, 2.0, None, ALU.add))
                link(nc.vector.reciprocal(den, den))
                link(nc.vector.tensor_tensor(s_, e, den, ALU.mult))
                link(nc.vector.tensor_tensor(s2, s_, s_, ALU.mult))
                terms = [1.0 / (2 * k + 1) for k in range(9)]
                link(nc.vector.tensor_scalar(acc, s2, terms[8], terms[7], ALU.mult, ALU.add))
                for c in terms[6::-1]:
                    link(nc.vector.tensor_tensor(acc, acc, s2, ALU.mult))
                    link(nc.vector.tensor_scalar(acc, acc, c, None, ALU.add))
                link(nc.vector.tensor_tensor(acc, acc, s_, ALU.mult))
                link(nc.vector.tensor_scalar(den, lam, 0.0, 2.0, ALU.min, ALU.mult))
                nc.vector.scalar_tensor_tensor(ls4, acc, -4.0, den, ALU.mult, ALU.add).then_inc(lam_ready, 1)

            def scale_out(n):
                dve.wait_ge(sq_done, w.n["sq"])
                cs = slice(n * NW, (n + 1) * NW)
                if n == 0:
                    dve.wait_ge(in_g2, 16)
                for t in range(NT):
                    ins = nc.vector.tensor_tensor(h2[:, t, cs], h2[:, t, cs], g_row2[:, cs], ALU.mult)
                ins.then_inc(out_scaled, 1)

            def jobs(hi, lo, v, *quads):
                return [lambda q=q: job_lo(q, hi, lo, cols[:, v:v + KC]) for q in quads]

            def mem_factors():
                dve.wait_ge(sq_done, NT)
                root(sumsq_m, 0)
                factors("mem")
                w.n["sq"] = NT

            def x_factors():
                dve.wait_ge(sq_done, 2 * NT)
                dve.wait_ge(in_tables, 16)
                root(sumsq_x, 1)
                factors("x")
                w.n["sq"] = 2 * NT

            def u_factors():
                dve.wait_ge(sq_done, w.n["sq"])
                sum_up(sums_a[:, :, :])
                root(sum_ab, 2)
                sum_up(sums_b[:, :, :])
                root(sum_ab, 3, r_first)
                link(nc.vector.tensor_tensor(R["u"]["r"], R["u"]["r"], r_first, ALU.mult))
                factors("u")

            def second_input():
                for t in range(NT):
                    ins = nc.vector.scalar_tensor_tensor(x1[:, t], x1[:, t], r_first[:, t:t + 1], g_row1[:, :], ALU.mult, ALU.mult)
                ins.then_inc(h_made, 1)

            def last_factors(name, k):
                dve.wait_ge(sq_done, w.n["sq"])
                sum_up(sums_a[:, :, :])
                root(sum_ab, k)
                factors(name)

            dve.wait_ge(vec_ps, 1)
            nc.vector.tensor_copy(cols[:, 0:V_END], bank(0, 0, V_END)).then_inc(cols_ready, 1)
            dve.wait_ge(cols_ready, 1)
            nc.vector.tensor_scalar(gn_half, cols[:, V_GN:V_GN + 8], 0.5, None, ALU.mult)
            link(nc.vector.tensor_scalar(gab_half[:, 0:16], cols[:, V_GAB:V_GAB + 16], 0.5, None, ALU.mult))
            four = tiles_memkv()
            four[0]["dve_hooks"] = {0: jobs(memT_hi, memT_lo, V_MEM, 1), 2: jobs(memT_hi, memT_lo, V_MEM, 2),
                                    3: jobs(memT_hi, memT_lo, V_MEM, 3), 7: [mem_factors]}
            for n in (2, 3):
                four[n]["dve_hooks"] = {6: jobs(xT_hi, xT_lo, V_IN, 2 * n - 4), 7: jobs(xT_hi, xT_lo, V_IN, 2 * n - 3)}
            last = four[3]["dve_hooks"].pop(7)
            four[2]["dve_hooks"][1] = [x_factors]
            job_lo(0, memT_hi, memT_lo, cols[:, V_MEM:V_MEM + KC])
            prev = chain(four, None)
            log_sigmoid()
            tiles = tiles_attention()
            tiles[0]["dve_hooks"] = {1: last}
            prev = chain(tiles, prev)
            prev = chain(tiles_merge(0, first=True), prev)
            w.rounds(dve, NG - 1, lambda i: chain(tiles_merge(i + 1), merge_last(i)))
            prev = merge_last(NG - 1)
            for k in range(NG // 2):
                tiles = res_tiles(w_out, "m", x1, k, what="u")
                if k == 0:
                    tiles[1]["dve_hooks"] = {2: [lambda: dve.wait_ge(in_res, 16 * NT),
                                                 lambda: dve.wait_ge(in_g1, 16)]}
                prev = chain(tiles, prev)
            tiles = tiles_two()
            tiles[1]["dve_hooks"] = {1: [u_factors], 6: [second_input]}
            prev = chain(tiles, prev)
            tiles = tiles_out2()
            tail_hooks(tiles, "dve_hooks", {
                4: [lambda: ret_decay(4)], 5: [lambda: ret_norm(4)],
                7: [lambda: ret_decay(5), lambda: ret_lo(4)], 8: [lambda: ret_norm(5)],
                10: [lambda: ret_decay(6), lambda: ret_lo(5)], 11: [lambda: ret_norm(6)],
                13: [lambda: ret_decay(7), lambda: ret_lo(6)], 14: [lambda: ret_norm(7), lambda: ret_lo(7), lambda: dve.wait_ge(in_h2, 16 * NT)]})
            prev = chain(tiles, prev)
            tiles = tiles_ffn(0)
            tiles[1]["dve_hooks"] = {1: [lambda: last_factors("u2", 4)]}
            chain(tiles, prev)
            w.rounds(dve, NF - 1, lambda i: chain(tiles_ffn(i + 1), ffn_last(i)))
            prev = ffn_last(NF - 1)
            for k in range(NG // 2):
                prev = chain(res_tiles(w_down, "ff", h2, k, FC // 2, "out"), prev)
            post(prev, 0, x_added)
            w.step("sq")
            scale_out(NG - 1)
            dve.wait_ge(sq_done, w.n["sq"])
            sum_up(sums_a[:, :, :])
            root(sum_ab, 5)
            for m in range(2):
                c = slice(m * D // 2, (m + 1) * D // 2)
                nc.vector.tensor_scalar(h2[:, 0, c], h2[:, 0, c], R["out"]["r"][:, 0:1], None, ALU.mult).then_inc(out_made[0], 1)

        @block.tensor
        def _(pe):
            w = Walk()
            pe.sem_inc(w_used, SLOTS)

            def transposes(src, dst, n):
                for c in range(n):
                    for t in range(NT):
                        o = dst + c * S + t * P
                        ins = nc.tensor.transpose(ps[:, o:o + P], src(t, c), ident)
                return ins

            def job(q, src, arrived):
                pair = q % 2
                for s in arrived:
                    pe.wait_ge(s, 16)
                if w.n[f"j{pair}"]:
                    pe.wait_ge(tx_free[pair], w(f"j{pair}"))
                transposes(lambda t, c: src[:, t, (q * QUAD + c) * P:(q * QUAD + c + 1) * P], (4 + 2 * pair) * NW, QUAD)\
                    .then_inc(tx_done[pair], 1)
                w.step(f"j{pair}", f"h{pair}")

            def parts_ready(q):
                pe.wait_ge(tx_free[q % 2], quads[q])

            quads = {}

            def unit_scores(unit):
                u = w.n["u"]
                if u:
                    pe.wait_ge(u_lo, u)
                pe.wait_ge(tx_free[0], w.n["j0"])
                pe.wait_ge(tx_free[1], w.n["j1"])
                for t in range(NT):
                    o = unit["s_at"][t]
                    for (qs, ks, _), kt in unit["blocks"][t]:
                        for n, ((qT, qc), (kT, kc)) in enumerate(zip(qs, ks)):
                            ins = nc.tensor.matmul(ps[:, o:o + P], qT[:, qc, t * P:(t + 1) * P], kT[:, kc, kt * P:(kt + 1) * P],
                                                   start=n == 0, stop=n == len(qs) - 1)
                        o += P
                ins.then_inc(u_score, 1)

            def unit_turn(unit):
                pe.wait_ge(u_exp, w("u", 1))
                for t in range(NT):
                    a, n = sb_at(unit, t)
                    for c in range(0, n, P):
                        o = unit["p_at"][t] + c
                        ins = nc.tensor.transpose(ps[:, o:o + P], scores[:, a + c:a + c + P], ident)
                ins.then_inc(u_pT, 1)

            def unit_values(unit):
                pe.wait_ge(u_pTc, w("u", 1))
                width = unit["width"]
                for t in range(NT):
                    a, _ = sb_at(unit, t)
                    blocks = unit["blocks"][t]
                    for n, ((_, _, v), kt) in enumerate(blocks):
                        o = unit["o_at"] + t * width
                        ins = nc.tensor.matmul(ps[:, o:o + width], probsT[:, a + n * P:a + (n + 1) * P], v(kt),
                                               start=n == 0, stop=n == len(blocks) - 1)
                ins.then_inc(u_out, 1)

            def unit_y(unit):
                pe.wait_ge(u_y, w("u", 1))
                transposes(lambda t, c: y_tok[:, t, c * P:(c + 1) * P], unit["y_at"], unit["width"] // P).then_inc(u_yT, 1)
                w.step("u")

            def ret_scores(n):
                if n:
                    pe.wait_ge(r_dec, n)
                if 0 < n <= QUAD:
                    pe.wait_ge(r_lo, n)
                pe.wait_ge(tx_free[0], w.n["j0"])
                pe.wait_ge(tx_free[1], w.n["j1"])
                half, h = n // QUAD, n % QUAD
                q, k = qrT[half], krT[half]
                nc.tensor.matmul(bank(6, 0, S), k[:, h, 0:P], q[:, h, 0:S], start=True, stop=True)
                nc.tensor.matmul(bank(6, S, S + P), k[:, h, P:S], q[:, h, P:S], start=True, stop=True).then_inc(r_score, 1)

            def ret_values(n):
                pe.wait_ge(r_dec, n + 1)
                if n > QUAD:
                    pe.wait_ge(r_y, n)
                if n < QUAD:
                    pe.wait_ge(l_tanh, min(n + 5, 8))
                half, h = n // QUAD, n % QUAD
                v = [vr[half][:, t, h * HD:(h + 1) * HD] for t in range(NT)]
                nc.tensor.matmul(bank(7, 0, HD), probsT[:, 0:P], v[0], start=True, stop=True)
                nc.tensor.matmul(bank(7, HD, 2 * HD), probsT[:, P:S], v[0], start=True, stop=False)
                nc.tensor.matmul(bank(7, HD, 2 * HD), probsT[:, S:S + P], v[1], start=False, stop=True).then_inc(r_out, 1)

            def ret_y(n):
                pe.wait_ge(r_y, n + 1)
                if n > QUAD:
                    pe.wait_ge(r_lo, n)
                if n == QUAD:
                    pe.wait_ge(tx_free[0], w.n["j0"])
                transposes(lambda t, c: y_tok[:, t, 0:HD], ret_y_bank(n) * NW, 1).then_inc(r_yT, 1)

            def lru_gates(n, heads):
                pe.wait_ge(l_conv, n + 1)
                if n == 0:
                    pe.wait_ge(in_gw, 32)
                    pe.wait_ge(tx_free[1], w.n["j1"])
                if heads:
                    pe.wait_ge(r_y, heads)
                nc.tensor.matmul(bank(7, 0, S), ga_w[:, n], lru_u, start=True, stop=True)
                nc.tensor.matmul(bank(7, S, 2 * S), gx_w[:, n], lru_u, start=True, stop=True).then_inc(l_gate, 1)

            def post(prev):
                if prev is None:
                    return
                w.count_post(prev)
                if through_stage(prev["post"]):
                    pe.wait_ge(st_ready, w("st", 1))
                    if w.n["j0"]:
                        pe.wait_ge(tx_free[0], w("j0"))
                    kind = prev["post"]
                    src, c0 = (kind[1], kind[2] * QUAD) if kind[0] == "res" and kind[3] == "u2" else (stage, 0)
                    transposes(lambda t, c: src[:, t, (c0 + c) * P:(c0 + c + 1) * P], 4 * NW, QUAD).then_inc(tx_done[0], 1)
                w.count_job(prev)

            def run(tile, prev):
                par, hcs, per, k0 = tile["par"], tile.get("hcs", HCS), tile.get("per", 2), tile.get("k0", 0)
                hi, lo = PARTS[tile["x"]]
                unit, need, hooks = tile.get("unit"), tile.get("need", {}), tile.get("pe_hooks", {})
                if w.n[f"a{par}"]:
                    pe.wait_ge(acc_free[par], w(f"a{par}"))
                at_ = (0, 1, 2, 3) if hcs == 4 else (0, 2, 4, 5)
                for i, h in enumerate(chunks(tile)):
                    s = w.n["g"] % SLOTS
                    for f in need.get(h, ()):
                        f()
                    pe.wait_ge(lo_ready, w("g", SLOTS + 1))
                    for k in range(per):
                        kc = h * per + k
                        first, last = kc == 0, kc == hcs * per - 1
                        for t in range(NT):
                            x_hi, x_lo = (m[:, k0 + kc, t * P:(t + 1) * P] for m in (hi, lo))
                            nc.tensor.matmul(bank(2 * par + t), x_hi, w_hi[:, s, k], start=first, stop=False)
                            nc.tensor.matmul(bank(2 * par + t), x_hi, w_lo[:, s, k], start=False, stop=False)
                            ins = nc.tensor.matmul(bank(2 * par + t), x_lo, w_hi[:, s, k], start=False, stop=last)
                    ins.then_inc(w_used, 1)
                    w.step("g")
                    if unit and h in at_:
                        (unit_scores, unit_turn, unit_values, unit_y)[at_.index(h)](unit)
                    if "ret" in tile and h == 0:
                        ret_scores(tile["ret"])
                    if "lru" in tile and h == 1:
                        lru_gates(tile["lru"], tile.get("ret", 0))
                    if i == pos(tile, 5 if unit else 3):
                        post(prev)
                    if "ret" in tile and h == 4:
                        ret_values(tile["ret"])
                    if "ret" in tile and h == 6:
                        ret_y(tile["ret"])
                    for f in hooks.get(i, ()):
                        f()
                return tile

            def chain(tiles, prev):
                for n, tile in enumerate(tiles):
                    tile.setdefault("par", n % 2)
                    prev = run(tile, prev if tile.get("follow", True) else None)
                return prev

            def begin(tile, src, in_):
                for q in range(QUAD):
                    quads[q] = w.n[f"j{q % 2}"] + q // 2 + 1
                for q in range(2):
                    job(q, src, [in_[q]])
                tile["pe_hooks"] = {q - 2: [lambda q=q: job(q, src, [in_[q]])] for q in (2, 3)}
                tile["need"] = {2 * q: [lambda q=q: parts_ready(q)] for q in range(QUAD)}

            pe.wait_ge(in_const, 16)
            pe.wait_ge(in_vec, 32)
            nc.tensor.transpose(bank(0, 0, P), vec_a[:, :], ident)
            nc.tensor.transpose(bank(0, P, V_END), vec_b[0:V_END - P, :], ident[0:V_END - P, 0:V_END - P]).then_inc(vec_ps, 1)
            four = tiles_memkv()
            begin(four[0], mem_tok, in_mem)
            four[0]["need"][0].append(lambda: pe.wait_ge(cols_ready, 1))
            for n in (2, 3):
                four[n]["pe_hooks"] = {k: [lambda q=q: job(q, x_tok, in_x)] for k, q in ((4, 2 * (n - 2)), (5, 2 * (n - 2) + 1))}
            prev = chain(four, None)
            tiles = tiles_attention()
            tiles[0]["need"] = {0: [lambda: pe.wait_ge(tx_free[0], w.n["j0"] - 1), lambda: pe.wait_ge(tx_free[1], w.n["j1"] - 1)],
                                4: [lambda: pe.wait_ge(tx_free[0], w.n["j0"])],
                                6: [lambda: pe.wait_ge(tx_free[1], w.n["j1"])]}
            prev = chain(tiles, prev)
            tiles = tiles_merge(0, first=True)
            for k, units in ((3, 4), (4, 12), (5, 16)):
                tiles[k]["need"] = {0: [lambda units=units: pe.wait_ge(u_lo, units)]}
            prev = chain(tiles, prev)
            w.rounds(pe, NG - 1, lambda i: chain(tiles_merge(i + 1), merge_last(i)))
            prev = merge_last(NG - 1)

            def quads_ready():
                pe.wait_ge(tx_free[0], w.n["j0"])

            for k in range(NG // 2):
                tiles = res_tiles(w_out, "m", x1, k, what="u")
                if k == 0:
                    tiles[0]["need"] = {0: [quads_ready], 6: [quads_ready]}
                prev = chain(tiles, prev)
            tiles = tiles_two()
            tiles[0]["need"] = {0: [quads_ready], 6: [quads_ready]}
            prev = chain(tiles, prev)
            tiles = tiles_out2()
            tiles[0]["need"] = {0: [lambda: pe.wait_ge(l_lo, 8)], 4: [lambda: pe.wait_ge(r_lo, 4)]}
            tiles[2]["need"] = {6: [lambda: pe.wait_ge(r_lo, 6)]}
            tiles[4]["need"] = {7: [lambda: pe.wait_ge(r_lo, 8)]}
            tail_hooks(tiles, "pe_hooks", {
                0: [lambda: ret_scores(4)], 1: [lambda: ret_values(4)],
                3: [lambda: ret_y(4), lambda: ret_scores(5)], 4: [lambda: ret_values(5)],
                6: [lambda: ret_y(5), lambda: ret_scores(6)], 7: [lambda: ret_values(6)],
                9: [lambda: ret_y(6), lambda: ret_scores(7)], 10: [lambda: ret_values(7)], 12: [lambda: ret_y(7)]})
            prev = chain(tiles, prev)
            tiles = tiles_ffn(0)
            tiles[0]["need"] = {0: [quads_ready], 6: [quads_ready]}
            chain(tiles, prev)
            w.rounds(pe, NF - 1, lambda i: chain(tiles_ffn(i + 1), ffn_last(i)))
            prev = ffn_last(NF - 1)
            for k in range(NG // 2):
                tiles = res_tiles(w_down, "ff", h2, k, FC // 2, "out")
                if k == 0:
                    tiles[0]["need"] = {0: [quads_ready], FC // 2 - 2: [quads_ready]}
                prev = chain(tiles, prev)


def shape_tables():
    f32 = np.float32
    half = HD // 2
    freq = (f32(10000.0) ** (-np.arange(half, dtype=f32) / f32(half))).astype(f32)
    angle = (np.arange(S, dtype=f32)[:, None] * freq[None, :]).astype(f32).astype(np.float64)
    cos, sin = np.cos(angle), np.sin(angle)
    c = np.zeros((P, C_END), f32)
    c[:, C_ID:C_ID + P] = np.eye(P)
    row, col = np.arange(P)[:, None], np.arange(P)[None, :]
    for t in range(NT):
        c[:, C_COS + t * half:C_COS + (t + 1) * half] = cos[t * P:(t + 1) * P]
        c[:, C_SIN + t * HD:C_SIN + t * HD + half] = -sin[t * P:(t + 1) * P]
        c[:, C_SIN + t * HD + half:C_SIN + (t + 1) * HD] = sin[t * P:(t + 1) * P]
    causal = col <= row
    same = [(row - col) % d == 0 for d in (4, 16)]
    seen = [np.ones((P, P), bool), causal, col >= row, causal,
            same[0], causal & same[0], same[1], causal & same[1]]
    for m, ok in enumerate(seen):
        c[:, C_MASK + m * P:C_MASK + (m + 1) * P] = np.where(ok, 0.0, -1e30)
    log_gamma = np.log1p(-np.exp2(-5.0 - np.arange(8)))
    ahead = np.arange(S)[None, :] - np.arange(P)[:, None]
    decay = np.where(ahead >= 0, np.exp(log_gamma[:, None, None] * np.maximum(ahead, 0)), 0.0) * HD ** -0.5
    return c, np.ascontiguousarray(decay.transpose(1, 0, 2)).astype(f32)


_IN = ("x", "mem", "w_in", "w_mem_kv", "w_proj_a", "w_proj_b", "w_proj_m", "w_out", "norm_final_g", "w_in_2", "w_out_2",
       "w_ffn_gate_2", "w_ffn_up_2", "w_ffn_down_2", "final_norm_w_2", "gate_a_w_2", "gate_x_w_2")
_VEC = ("norm_mem_g", "norm_in_g", "ln1_w_2", "ln2_w_2", "ret_gn_w_2", "conv_w_2", "conv_b_2", "gate_a_b_2", "gate_x_b_2",
        "lru_lambda_2")


def kernel(**inputs):
    import concourse.bacc as bacc
    from concourse.bass_utils import run_bass_kernel_spmd

    nc = bacc.Bacc("TRN2", target_bir_lowering=False, num_devices=1)
    arrays, args = {}, []

    def give(name, a):
        arrays[name] = a
        args.append(nc.dram_tensor(name, a.shape, mybir.dt.from_np(a.dtype), kind="ExternalInput").ap())

    for name in _IN:
        a = np.ascontiguousarray(inputs[name])
        while a.ndim > 1 and a.shape[0] == 1:
            a = a[0]
        give(f"in_{name}", a)
    give("in_vectors", np.concatenate([np.asarray(inputs[name]).reshape(-1, P) for name in _VEC]))
    consts, decay = shape_tables()
    give("in_consts", consts)
    give("in_decay", decay)
    args.append(nc.dram_tensor("h_spill", (S, D), F32, kind="Internal").ap())
    args.append(nc.dram_tensor("out_dram", (S, D), F32, kind="ExternalOutput").ap())
    build(nc, *args)
    r = run_bass_kernel_spmd(nc, [arrays], core_ids=[0])
    return r.results[0]["out_dram"].reshape(1, S, D)
```
